# Optimizing a Trainium2 kernel written in Bass

```python
import functools
import jax, jax.numpy as jnp
from jax import lax
import numpy as np

D_MODEL = 1024
BATCH = 1
SEQ = 512
DEPTH = 2
DEC_BATCH = 8
DEC_SEQ = 8
PAST_LEN = 256
PAGE_SIZE = 128

N_HEADS_A = 8
HEAD_DIM_A = 64
WIDTH_A = N_HEADS_A * HEAD_DIM_A
Q_BLOCK = 128
WIDTH_B = 512
N_BLOCKS_B = 8
BLOCK_B = WIDTH_B // N_BLOCKS_B
CONV_B = 4
LRU_C = 8.0
WIDTH_C = 512
CONV_C = 3
N_BRANCH = 3
FFN_HIDDEN = 2816
RMS_EPS = 1e-6
IN_SIZES = (WIDTH_A, WIDTH_A, WIDTH_A, N_HEADS_A, WIDTH_B, WIDTH_B, WIDTH_C, WIDTH_C, WIDTH_C, N_BRANCH * D_MODEL)
N_IN = 3 * WIDTH_A + N_HEADS_A + 2 * WIDTH_B + 3 * WIDTH_C + N_BRANCH * D_MODEL
N_MIX = WIDTH_A + WIDTH_B + WIDTH_C

kernel_name = 'fox_rglru_shortconv_macaron_step'

def rms_norm(x, g):
    xf = x.astype(jnp.float32)
    y = xf * lax.rsqrt(jnp.mean(xf * xf, axis=-1, keepdims=True) + RMS_EPS)
    return (y * g.astype(jnp.float32)).astype(x.dtype)

def swiglu(x, w_in, w_out):
    gate, up = jnp.split(x @ w_in, 2, axis=-1)
    return (jax.nn.silu(gate) * up) @ w_out

def split_columns(z):
    parts = []
    start = 0
    for size in IN_SIZES:
        parts.append(z[..., start:start + size])
        start += size
    return parts

def fox_attend(q, k, v, cq, ck, q_pos, k_pos):
    s = jnp.einsum('nqhd,nkhd->nhqk', q, k).astype(jnp.float32) * (HEAD_DIM_A ** -0.5)
    s = s + jnp.transpose(cq, (0, 2, 1))[:, :, :, None] - jnp.transpose(ck, (0, 2, 1))[:, :, None, :]
    mask = k_pos[None, :] <= q_pos[:, None]
    s = jnp.where(mask, s, -jnp.inf)
    p = jax.nn.softmax(s, axis=-1)
    return jnp.einsum('nhqk,nkhd->nqhd', p.astype(v.dtype), v)

def fox_prompt(q, k, v, logf):
    n, t, h, d = q.shape
    c = jnp.cumsum(logf, axis=1)
    nb = t // Q_BLOCK
    k_pos = jnp.arange(t)
    qb = jnp.moveaxis(q.reshape(n, nb, Q_BLOCK, h, d), 1, 0)
    cqb = jnp.moveaxis(c.reshape(n, nb, Q_BLOCK, h), 1, 0)
    starts = jnp.arange(nb) * Q_BLOCK

    def block(args):
        qi, cqi, s0 = args
        return fox_attend(qi, k, v, cqi, c, s0 + jnp.arange(Q_BLOCK), k_pos)

    o = lax.map(block, (qb, cqb, starts))
    return jnp.moveaxis(o, 0, 1).reshape(n, t, h * d)

def fox_sample(q, k, v, logf, past_k, past_v, past_logf):
    n, t, h, d = q.shape
    p = past_k.shape[1]
    k_all = jnp.concatenate([past_k.astype(k.dtype), k], axis=1)
    v_all = jnp.concatenate([past_v.astype(v.dtype), v], axis=1)
    c = jnp.cumsum(jnp.concatenate([past_logf.astype(jnp.float32), logf], axis=1), axis=1)
    o = fox_attend(q, k_all, v_all, c[:, p:], c, p + jnp.arange(t), jnp.arange(p + t))
    return o.reshape(n, t, h * d)

def causal_dwconv(u, buf, w):
    kw = w.shape[0]
    t = u.shape[1]
    up = jnp.concatenate([buf.astype(u.dtype), u], axis=1)
    out = w[0] * up[:, 0:t]
    for j in range(1, kw):
        out = out + w[j] * up[:, j:j + t]
    return out, up[:, up.shape[1] - (kw - 1):]

def rg_lru(xc, h0, wa, ba, wx, bx, lam):
    n, t, w = xc.shape
    xb = xc.reshape(n, t, N_BLOCKS_B, BLOCK_B)
    r = jax.nn.sigmoid(jnp.einsum('ntgi,gij->ntgj', xb, wa).reshape(n, t, w) + ba).astype(jnp.float32)
    i = jax.nn.sigmoid(jnp.einsum('ntgi,gij->ntgj', xb, wx).reshape(n, t, w) + bx).astype(jnp.float32)
    log_a = -LRU_C * r * jax.nn.softplus(-lam.astype(jnp.float32))
    a = jnp.exp(log_a)
    b = jnp.sqrt(-jnp.expm1(2.0 * log_a)) * (i * xc.astype(jnp.float32))
    b = b.at[:, 0].add(a[:, 0] * h0.astype(jnp.float32))

    def combine(left, right):
        a1, b1 = left
        a2, b2 = right
        return a1 * a2, a2 * b1 + b2

    _, h = lax.associative_scan(combine, (a, b), axis=1)
    return h.astype(xc.dtype), h[:, -1].astype(xc.dtype)

def hybrid_layer(x, p, attn_fn, lru_h0, lru_buf, sc_buf):
    x = x + 0.5 * swiglu(rms_norm(x, p['ffn1_norm']), p['ffn1_w_in'], p['ffn1_w_out'])
    h = rms_norm(x, p['mix_norm'])
    n, t, _ = h.shape
    q, k, v, f, bx_in, by_in, sb, sc, sx, g = split_columns(h @ p['w_in'])
    q = rms_norm(q.reshape(n, t, N_HEADS_A, HEAD_DIM_A), p['q_norm'])
    k = rms_norm(k.reshape(n, t, N_HEADS_A, HEAD_DIM_A), p['k_norm'])
    v = v.reshape(n, t, N_HEADS_A, HEAD_DIM_A)
    logf = jax.nn.log_sigmoid((f + p['b_forget']).astype(jnp.float32))
    o_a = attn_fn(q, k, v, logf)
    xc, lru_buf_new = causal_dwconv(bx_in, lru_buf, p['lru_conv_w'])
    xc = xc + p['lru_conv_b']
    hb, h_last = rg_lru(xc, lru_h0, p['lru_wa'], p['lru_ba'], p['lru_wx'], p['lru_bx'], p['lru_lambda'])
    o_b = hb * jax.nn.gelu(by_in)
    uc, sc_buf_new = causal_dwconv(sc * sx, sc_buf, p['sc_conv_w'])
    o_c = sb * uc
    wb = p['w_branch']
    gates = jax.nn.sigmoid(g.reshape(n, t, N_BRANCH, D_MODEL))
    merged = (gates[:, :, 0] * (o_a @ wb[:WIDTH_A])
              + gates[:, :, 1] * (o_b @ wb[WIDTH_A:WIDTH_A + WIDTH_B])
              + gates[:, :, 2] * (o_c @ wb[WIDTH_A + WIDTH_B:]))
    x = x + merged @ p['w_out']
    x = x + 0.5 * swiglu(rms_norm(x, p['ffn2_norm']), p['ffn2_w_in'], p['ffn2_w_out'])
    return x, (k, v, logf, h_last, lru_buf_new, sc_buf_new)

def setup_inputs(seed: int = 0) -> dict:
    key = jax.random.key(seed)
    ks = iter(jax.random.split(key, 48))

    def nrm(shape, scale):
        return jax.random.normal(next(ks), shape, jnp.float32) * scale

    def gain(shape):
        return 1.0 + nrm(shape, 0.02)

    n_pages = PAST_LEN // PAGE_SIZE
    n_used = DEC_BATCH * n_pages
    n_phys = n_used + n_used // 4
    page_table = jax.random.permutation(next(ks), n_phys)[:n_used].reshape(DEC_BATCH, n_pages).astype(jnp.int32)
    u = jax.random.uniform(next(ks), (DEPTH, WIDTH_B), jnp.float32, minval=0.9, maxval=0.999)
    a0 = u ** (1.0 / LRU_C)
    lru_lambda = jnp.log(a0) - jnp.log1p(-a0)
    b_forget = jax.random.uniform(next(ks), (DEPTH, N_HEADS_A), jnp.float32, minval=1.0, maxval=6.0)
    return {
        'x_prompt': nrm((BATCH, SEQ, D_MODEL), 1.0),
        'x_sample': nrm((DEC_BATCH, DEC_SEQ, D_MODEL), 1.0),
        'cache_k': nrm((n_phys, DEPTH, PAGE_SIZE, N_HEADS_A, HEAD_DIM_A), 1.0),
        'cache_v': nrm((n_phys, DEPTH, PAGE_SIZE, N_HEADS_A, HEAD_DIM_A), 1.0),
        'cache_logf': jax.nn.log_sigmoid(nrm((n_phys, DEPTH, PAGE_SIZE, N_HEADS_A), 1.0) + 4.0),
        'state_lru_h': nrm((DEC_BATCH, DEPTH, WIDTH_B), 0.5),
        'state_lru_conv': nrm((DEC_BATCH, DEPTH, CONV_B - 1, WIDTH_B), 1.0),
        'state_sc_conv': nrm((DEC_BATCH, DEPTH, CONV_C - 1, WIDTH_C), 1.0),
        'page_table': page_table,
        'ffn1_norm': gain((DEPTH, D_MODEL)),
        'ffn1_w_in': nrm((DEPTH, D_MODEL, 2 * FFN_HIDDEN), D_MODEL ** -0.5),
        'ffn1_w_out': nrm((DEPTH, FFN_HIDDEN, D_MODEL), FFN_HIDDEN ** -0.5),
        'mix_norm': gain((DEPTH, D_MODEL)),
        'w_in': nrm((DEPTH, D_MODEL, N_IN), D_MODEL ** -0.5),
        'b_forget': b_forget,
        'q_norm': gain((DEPTH, HEAD_DIM_A)),
        'k_norm': gain((DEPTH, HEAD_DIM_A)),
        'lru_conv_w': nrm((DEPTH, CONV_B, WIDTH_B), CONV_B ** -0.5),
        'lru_conv_b': nrm((DEPTH, WIDTH_B), 0.01),
        'lru_wa': nrm((DEPTH, N_BLOCKS_B, BLOCK_B, BLOCK_B), BLOCK_B ** -0.5),
        'lru_ba': nrm((DEPTH, WIDTH_B), 0.01),
        'lru_wx': nrm((DEPTH, N_BLOCKS_B, BLOCK_B, BLOCK_B), BLOCK_B ** -0.5),
        'lru_bx': nrm((DEPTH, WIDTH_B), 0.01),
        'lru_lambda': lru_lambda,
        'sc_conv_w': nrm((DEPTH, CONV_C, WIDTH_C), CONV_C ** -0.5),
        'w_branch': nrm((DEPTH, N_MIX, D_MODEL), WIDTH_A ** -0.5),
        'w_out': nrm((DEPTH, D_MODEL, D_MODEL), D_MODEL ** -0.5),
        'ffn2_norm': gain((DEPTH, D_MODEL)),
        'ffn2_w_in': nrm((DEPTH, D_MODEL, 2 * FFN_HIDDEN), D_MODEL ** -0.5),
        'ffn2_w_out': nrm((DEPTH, FFN_HIDDEN, D_MODEL), FFN_HIDDEN ** -0.5),
    }

def reference(x_prompt, x_sample, cache_k, cache_v, cache_logf, state_lru_h, state_lru_conv, state_sc_conv,
              page_table, ffn1_norm, ffn1_w_in, ffn1_w_out, mix_norm, w_in, b_forget, q_norm, k_norm,
              lru_conv_w, lru_conv_b, lru_wa, lru_ba, lru_wx, lru_bx, lru_lambda, sc_conv_w, w_branch, w_out,
              ffn2_norm, ffn2_w_in, ffn2_w_out):
    n_prompt = x_prompt.shape[0]
    n_dec = page_table.shape[0]
    zero_h = jnp.zeros((n_prompt, WIDTH_B), x_prompt.dtype)
    zero_lru_buf = jnp.zeros((n_prompt, CONV_B - 1, WIDTH_B), x_prompt.dtype)
    zero_sc_buf = jnp.zeros((n_prompt, CONV_C - 1, WIDTH_C), x_prompt.dtype)
    yp = x_prompt
    ys = x_sample
    pk, pv, plf, ph, pcb, psb = [], [], [], [], [], []
    sk, sv, slf, sh, scb, ssb = [], [], [], [], [], []
    for l in range(DEPTH):
        p = {
            'ffn1_norm': ffn1_norm[l], 'ffn1_w_in': ffn1_w_in[l], 'ffn1_w_out': ffn1_w_out[l],
            'mix_norm': mix_norm[l], 'w_in': w_in[l], 'b_forget': b_forget[l],
            'q_norm': q_norm[l], 'k_norm': k_norm[l],
            'lru_conv_w': lru_conv_w[l], 'lru_conv_b': lru_conv_b[l],
            'lru_wa': lru_wa[l], 'lru_ba': lru_ba[l], 'lru_wx': lru_wx[l], 'lru_bx': lru_bx[l],
            'lru_lambda': lru_lambda[l], 'sc_conv_w': sc_conv_w[l],
            'w_branch': w_branch[l], 'w_out': w_out[l],
            'ffn2_norm': ffn2_norm[l], 'ffn2_w_in': ffn2_w_in[l], 'ffn2_w_out': ffn2_w_out[l],
        }
        yp, st = hybrid_layer(yp, p, fox_prompt, zero_h, zero_lru_buf, zero_sc_buf)
        pk.append(st[0]); pv.append(st[1]); plf.append(st[2]); ph.append(st[3]); pcb.append(st[4]); psb.append(st[5])
        past_k = cache_k[page_table, l].reshape(n_dec, -1, N_HEADS_A, HEAD_DIM_A)
        past_v = cache_v[page_table, l].reshape(n_dec, -1, N_HEADS_A, HEAD_DIM_A)
        past_lf = cache_logf[page_table, l].reshape(n_dec, -1, N_HEADS_A)
        attn_s = functools.partial(fox_sample, past_k=past_k, past_v=past_v, past_logf=past_lf)
        ys, st = hybrid_layer(ys, p, attn_s, state_lru_h[:, l], state_lru_conv[:, l], state_sc_conv[:, l])
        sk.append(st[0]); sv.append(st[1]); slf.append(st[2]); sh.append(st[3]); scb.append(st[4]); ssb.append(st[5])
    prompt_k = jnp.stack(pk, axis=1)
    prompt_v = jnp.stack(pv, axis=1)
    prompt_logf = jnp.stack(plf, axis=1)
    prompt_lru_h = jnp.stack(ph, axis=1)
    prompt_lru_conv = jnp.stack(pcb, axis=1)
    prompt_sc_conv = jnp.stack(psb, axis=1)
    sample_k = jnp.stack(sk, axis=1)
    sample_v = jnp.stack(sv, axis=1)
    sample_logf = jnp.stack(slf, axis=1)
    sample_lru_h = jnp.stack(sh, axis=1)
    sample_lru_conv = jnp.stack(scb, axis=1)
    sample_sc_conv = jnp.stack(ssb, axis=1)
    return (yp, ys, prompt_k, prompt_v, prompt_logf, prompt_lru_h, prompt_lru_conv, prompt_sc_conv,
            sample_k, sample_v, sample_logf, sample_lru_h, sample_lru_conv, sample_sc_conv)


_drawn_inputs = setup_inputs


def setup_inputs(seed=0):
    import zlib

    import numpy as np

    out = dict(_drawn_inputs(seed))
    spreads = {}
    factors = {'cache_logf': 17.692,
     'ffn1_norm': 3.71,
     'q_norm': 25.917,
     'k_norm': 2.885,
     'lru_ba': 24.319,
     'lru_bx': 8.0,
     'ffn2_norm': 5.517}
    for name, (base, spread) in spreads.items():
        noise = np.random.default_rng([zlib.crc32(name.encode()), seed]).standard_normal(out[name].shape)
        drawn = base * np.exp(spread * noise) if base else spread * noise
        out[name] = __import__('jax').numpy.asarray(drawn.astype(out[name].dtype))
    for name, factor in factors.items():
        out[name] = (out[name] * factor).astype(out[name].dtype)
    return out
```

```python
from contextlib import ExitStack

import concourse.bass as bass
import numpy as np
from concourse import mybir

F32 = mybir.dt.float32
F32R = mybir.dt.float32r
BF16 = mybir.dt.bfloat16
I32 = mybir.dt.int32
ALU = mybir.AluOpType
ACT = mybir.ActivationFunctionType
AX = mybir.AxisListType

P = 128
D = 1024
KD = D // P
DEPTH = 2
SEQ = 512
QB = SEQ // P
SB, ST = 8, 8
NS = SB * ST
N = SEQ + NS
HF = N // 2
H, HD = 8, 64
PAIRS = H // 2
WID = 512
FFN = 2816
EPS = 1e-6
PAGE = 128
NPG = 2
PAST = NPG * PAGE
N_IN = 3 * WID + H + 2 * WID + 3 * WID + 3 * D
COL_Q, COL_K, COL_V, COL_F = 0, WID, 2 * WID, 3 * WID
COL_BX = COL_F + H
COL_BY, COL_SB, COL_SC, COL_SX, COL_G = (COL_BX + WID * n for n in range(1, 6))
CONV_B, CONV_C = 4, 3
HB_, HC_ = CONV_B - 1, CONV_C - 1
STEP_B, STEP_C = HB_ + ST, HC_ + ST
UB, UC = HB_ + SEQ + SB * STEP_B, HC_ + SEQ + SB * STEP_C
XB, XCW = UB - HB_, UC - HC_
SB0, SC0 = HB_ + SEQ, HC_ + SEQ
R_CW, R_CB, R_BA, R_BX, R_LAM, R_SW, R_H0, R_CS, R_SS, NR = 0, 4, 5, 6, 7, 8, 11, 19, 43, 59
O_HP, O_CP, O_SP, O_HS, O_CS, O_SS, NO = 0, 1, 4, 6, 14, 38, 54
C_ID, C_ONE, C_BONE, C_IND, C_MREP, C_REP, C_SEL, C_M12 = 0, 128, 256, 384, 896, 960, 1088, 1104
C_KEEP = 1106
C_MD, C_MS = C_KEEP, C_KEEP + P
NCONST = C_KEEP + 2 * P
NEG = -1e30
F_W = 2 * H


class Stage:

    def __init__(self, plan, steps, units, tiles):
        assert steps == 1 or (units % 2 == 0 and tiles % 4 == 0)
        self.steps, self.units, self.tiles = steps, units, tiles
        self.first_unit, self.first_tile = plan["units"], plan["tiles"]
        plan["units"] += steps * units
        plan["tiles"] += steps * tiles
        self.plan = plan

    def slot(self, k):
        return (self.first_tile + k) % 4

    def turn(self, k, layer, step=0):
        whole = self.plan["layer_tiles"] // 4
        return layer * whole + step * (self.tiles // 4) + (self.plan["before"] + self.first_tile + k) // 4

    def unit(self, k, layer, step=0):
        return layer * self.plan["layer_units"] + step * self.units + self.first_unit + k

    def unit_slot(self, k):
        return (self.first_unit + k) % 2


AHEAD = 3
PRE_TILES = 12


def make_plan():
    plan = {"units": 0, "tiles": 0, "before": PRE_TILES, "layer_tiles": 0, "layer_units": 0}
    s = {}

    def ffn(name):
        s[name + "norm"] = Stage(plan, 1, 0, 1)
        s[name] = []
        for pairs in (4, 4, 3):
            s[name].append((Stage(plan, pairs, 2, 4), Stage(plan, 2, 2, 4), 2 * pairs))

    ffn("ffn1")
    s["mixnorm"] = Stage(plan, 1, 0, 1)
    s["fv"] = Stage(plan, 1, 2, 8)
    s["pair"] = Stage(plan, PAIRS, 4, 24)
    s["state"] = Stage(plan, 1, 0, 1)
    s["merge"] = Stage(plan, 4, 6, 12)
    s["out"] = Stage(plan, 2, 2, 4)
    ffn("ffn2")
    plan["tiles_used"] = plan["tiles"]
    plan["tiles"] += -plan["tiles"] % 4
    plan["layer_tiles"], plan["layer_units"] = plan["tiles"], plan["units"]
    assert plan["units"] % 2 == 0
    return s, plan


def sequences(buf, first, step, at, n):
    return buf[:, first:first + SB * step].rearrange("p (s c) -> p s c", c=step)[:, :, at:at + n]


def one_each(buf, at):
    return buf[:, SB0:SB0 + SB * STEP_B].rearrange("p (s c) -> p s c", c=STEP_B)[:, :, at]


def build(nc, t_in, t_out):
    S, plan = make_plan()
    with ExitStack() as ctx:
        ctx.enter_context(nc.allow_non_contiguous_dma(reason="one value per partition: forget biases"))

        def sem(name):
            return ctx.enter_context(nc.semaphore(name))

        def sb(name, shape, dt=F32, where=ctx):
            return where.enter_context(nc.sbuf_tensor(name, shape, dt))

        ps = [ctx.enter_context(nc.psum_tensor(f"ps{i}", [P, 2, 512], F32)) for i in range(4)]

        x = sb("x", [P, KD, N])
        hh = sb("hh", [P, KD, N], F32R)
        hl = sb("hl", [P, KD, N], F32R)
        wraw = sb("wraw", [P, 2, KD * 256])
        whi = sb("whi", [P, 2, KD * P], F32R)
        wlo = sb("wlo", [P, 2, KD * P], F32R)
        const = sb("const", [P, C_KEEP])
        identb = sb("identb", [P, P], BF16)
        maskd = sb("maskd", [P, P], BF16)
        masks = sb("masks", [P, P], BF16)
        par_all = sb("par_all", [P, DEPTH, 4 * NR])
        gains = sb("gains", [P, DEPTH, 26])
        gain = sb("gain", [P, 26])
        bfor = sb("bfor", [F_W, DEPTH])
        bf = sb("bf", [F_W, 1])
        decay = sb("decay", [P, DEPTH, 2, 4])
        dk = sb("dk", [P, 2, 4])
        nbias = sb("nbias", [P, 2])
        eps = sb("eps", [P, 2])
        pages = sb("pages", [1, SB * NPG], I32)
        wfr = sb("wfr", [P, KD, F_W])
        wfh = sb("wfh", [P, KD * F_W + P - F_W], F32R)
        wfl = sb("wfl", [P, KD * F_W + P - F_W], F32R)
        wab = sb("wab", [P, 2, P])
        small = sb("small", [P, 64])
        tmp = [sb(f"tmp{i}", [P, UB + 1]) for i in range(7)]
        ident = const[:, C_ID:C_ID + P]
        ones = const[:, C_ONE:C_ONE + P]
        bones = const[:, C_BONE:C_BONE + P]

        with ExitStack() as m:
            ah = sb("ah", [P, 8, N], F32R, m)
            al = sb("al", [P, 8, N], F32R, m)
        with ExitStack() as m:
            xin = sb("xin", [P, 5, D], F32, m)
            rows = sb("rows", [NR, DEPTH, WID], F32, m)
            rowsg = sb("rowsg", [26, DEPTH, P], F32, m)
            cmask = sb("cmask", [P, 2 * P], F32, m)
            spt = [sb(f"spt{i}", [P, DEPTH, 4], F32, m) for i in range(5)]
        with ExitStack() as m:
            yout = sb("yout", [P, 5, D], F32, m)
        with ExitStack() as m:
            o = sb("o", [P, 12, N], F32, m)
            with ExitStack() as m2:
                kv = sb("kv", [P, SB * NPG, P], F32, m2)
                kpt = sb("kpt", [P, SB * PAST], F32, m2)
                prob = [sb(f"prob{i}", [P, 10 * P], F32, m2) for i in range(2)]
                probt = sb("probt", [P, 10 * P], F32, m2)
                probs = sb("probs", [P, 3 * P], F32, m2)
                probst = sb("probst", [P, 3 * P], F32, m2)
                qp = sb("qp", [P, N], F32, m2)
                kp = sb("kp", [P, N], F32, m2)
                cp = sb("cp", [96, SEQ], BF16, m2)
                ck = sb("ck", [96, SEQ], BF16, m2)
                cq = [sb(f"cq{i}", [96, SEQ], BF16, m2) for i in range(2)]
                rhss = sb("rhss", [P, 3 * P], F32, m2)
                lhss = sb("lhss", [P, P], F32, m2)
                qeo = [sb(f"qeo{i}", [P, P], F32, m2) for i in range(2)]
                cs = sb("cs", [P, PAST + ST], F32, m2)
                lfp = sb("lfp", [P, NPG, 2 * NS], F32, m2)
                lf = sb("lf", [F_W, N], F32, m2)
                vp = sb("vp", [P, 5, P], F32, m2)
                vtok = sb("vtok", [P, 5, WID], F32, m2)
                kout = sb("kout", [P, 5, P], F32, m2)
                lfo = sb("lfo", [P, 5, H], F32, m2)
                fcol = sb("fcol", [P, NO], F32, m2)
                fout = sb("fout", [P, 4, NO], F32, m2)
                prow = sb("prow", [P, NR], F32, m2)
            with ExitStack() as m2:
                oh = sb("oh", [P, 12, N], F32R, m2)
                merged = sb("merged", [P, KD, N], F32, m2)
                frow = sb("frow", [NO, WID], F32, m2)
        with ExitStack() as m:
            ol = sb("ol", [P, 12, N], F32R, m)

        in_loaded, pages_loaded = sem("in_loaded"), sem("pages_loaded")
        unit_loaded = [sem(f"unit_loaded{i}") for i in range(2)]
        hi_ready, lo_ready = sem("hi_ready"), sem("lo_ready")
        filled = [sem(f"filled{i}") for i in range(4)]
        freed = [sem(f"freed{i}") for i in range(4)]
        consts_ready = sem("consts_ready")
        pre_done = sem("pre_done")
        sq_ready, sq_added = sem("sq_ready"), sem("sq_added")
        hf_ready, hh_ready, h_ready = sem("hf_ready"), sem("hh_ready"), sem("h_ready")
        a_ready = sem("a_ready")
        wf_loaded, wf_hi, wf_ready = sem("wf_loaded"), sem("wf_hi"), sem("wf_ready")
        lfp_loaded, lfp_ready = sem("lfp_loaded"), sem("lfp_ready")
        absz_ready, expz_ready, logf_ready = sem("absz_ready"), sem("expz_ready"), sem("logf_ready")
        v_stored, k_stored, lf_stored, f_stored = sem("v_stored"), sem("k_stored"), sem("lf_stored"), sem("f_stored")
        cbias_ready = sem("cbias_ready")
        kv_loaded, wab_loaded = sem("kv_loaded"), sem("wab_loaded")
        qk_squared, qk_ready = sem("qk_squared"), sem("qk_ready")
        conv_in, xc_ready = sem("conv_in"), sem("xc_ready")
        max_ready, exp_ready, prob_ready = sem("max_ready"), sem("exp_ready"), sem("prob_ready")
        pv_done, vp_ready = sem("pv_done"), sem("vp_ready")
        gates_ready, root_in, root_ready = sem("gates_ready"), sem("root_in"), sem("root_ready")
        f_ready = sem("f_ready")
        oh_ready, o_ready = sem("oh_ready"), sem("o_ready")
        merged_ready, mh_ready, m_ready = sem("merged_ready"), sem("mh_ready"), sem("m_ready")
        y_stored = sem("y_stored")

        def wait_apart(eng, what, value):
            if not isinstance(value, int):
                value = eng.snap(value)
                eng.compute_val(value)
            eng.wait_ge(pre_done, 1)
            eng.wait_ge(what, value)

        def cols(k):
            return ps[k][:, :, 0:HF]

        def two(ap):
            return ap.rearrange("p (b n) -> p b n", b=2)

        def raw_tile(u, j, rowwise=False):
            if rowwise:
                return wraw[:, u, j * 4 * P:(j + 1) * 4 * P].rearrange("p (k c) -> p k c", c=P)
            return wraw[:, u, :].rearrange("p (k c) -> p k c", c=256)[:, :, j * P:(j + 1) * P]

        def split_tile(buf, j, rowwise=False):
            n = 4 if rowwise else KD
            return buf[:, j, 0:n * P].rearrange("p (k c) -> p k c", c=P)

        def ahead(st, k):
            k2 = k + 2
            rowwise = st is S["pair"] and k2 in (6, 7)
            return k2 // 2, k2 % 2, rowwise

        block = ctx.enter_context(nc.Block())

        @block.sync
        def _(sp):
            sp.dma_start(pages[:], t_in["page_table"].rearrange("s g -> (s g)").rearrange("(a n) -> a n", a=1)).then_inc(pages_loaded, 16)
            sp.dma_start(xin[:, 0:4, :], t_in["x_prompt"].rearrange("a (b p) d -> p (a b) d", p=P)).then_inc(in_loaded, 16)
            sp.dma_start(xin[0:NS, 4, :], t_in["x_sample"].rearrange("s t d -> (s t) d")).then_inc(in_loaded, 16)
            sp.dma_start(const[:, :], t_in["const_table"][:, 0:C_KEEP]).then_inc(in_loaded, 16)
            sp.dma_start(cmask[:, :], t_in["const_table"][:, C_KEEP:NCONST]).then_inc(in_loaded, 16)
            for l in range(DEPTH):
                for name, r, n in (("lru_conv_w", R_CW, CONV_B), ("sc_conv_w", R_SW, CONV_C)):
                    sp.dma_start(rows[r:r + n, l, :], t_in[name][l]).then_inc(in_loaded, 16)
                for name, r in (("lru_conv_b", R_CB), ("lru_ba", R_BA), ("lru_bx", R_BX), ("lru_lambda", R_LAM)):
                    sp.dma_start(rows[r:r + 1, l, :], t_in[name][l:l + 1, :]).then_inc(in_loaded, 16)
                sp.dma_start(rows[R_H0:R_H0 + SB, l, :], t_in["state_lru_h"][:, l, :]).then_inc(in_loaded, 16)
                for s in range(SB):
                    sp.dma_start(rows[R_CS + HB_ * s:R_CS + HB_ * (s + 1), l, :], t_in["state_lru_conv"][s, l]).then_inc(in_loaded, 16)
                    sp.dma_start(rows[R_SS + HC_ * s:R_SS + HC_ * (s + 1), l, :], t_in["state_sc_conv"][s, l]).then_inc(in_loaded, 16)
                for n, name in enumerate(("ffn1_norm", "mix_norm", "ffn2_norm")):
                    sp.dma_start(rowsg[8 * n:8 * n + 8, l, :], t_in[name][l].rearrange("(k p) -> k p", p=P)).then_inc(in_loaded, 16)
                for n, name in enumerate(("q_norm", "k_norm")):
                    for e in range(2):
                        sp.dma_start(rowsg[24 + n:25 + n, l, HD * e:HD * (e + 1)], t_in[name][l:l + 1, :]).then_inc(in_loaded, 16)
                for e in range(2):
                    sp.dma_start(bfor[H * e:H * (e + 1), l:l + 1], t_in["b_forget"][l].rearrange("(h a) -> h a", a=1)).then_inc(in_loaded, 16)

            def load(st, k, L, i, *parts):
                n = st.unit(k, L, i)
                u = st.unit_slot(k)
                sp.wait_ge(lo_ready, n * 2 - 2 + AHEAD)
                at = 0
                for name, k0, kc, c0, nc_ in parts:
                    src = t_in[name].rearrange("l (k p) n -> l p k n", p=P)[bass.ds(L, 1), :, k0:k0 + kc, bass.ds(c0, nc_)]
                    width = sum(q[4] for q in parts)
                    dst = wraw[:, u, 0:KD * width].rearrange("p (k c) -> p k c", c=width)[:, 0:kc, at:at + nc_]
                    sp.dma_start(dst, src.rearrange("l p k n -> p (l k) n")).then_inc(unit_loaded[u], 32 // len(parts))
                    at += nc_

            def ffn(name, L):
                w1, w2 = name + "_w_in", name + "_w_out"
                done = 0
                for st_in, st_out, kc in S[name]:
                    with sp.Fori(0, st_in.steps) as i:
                        load(st_in, 0, L, i, (w1, 0, KD, i * 256 + done * P, 256))
                        load(st_in, 1, L, i, (w1, 0, KD, i * 256 + (done * P + FFN), 256))
                    with sp.Fori(0, 2) as i:
                        for k in range(2):
                            load(st_out, k, L, i, (w2, done, kc, i * 512 + 256 * k, 256))
                    done += kc

            sp.wait_ge(pages_loaded, 16)
            with sp.Fori(0, DEPTH) as L:
                sp.wait_ge(wf_ready, L + 1)
                for e in range(2):
                    src = t_in["w_in"].rearrange("l (k p) n -> l p k n", p=P)[bass.ds(L, 1), :, :, COL_F:COL_F + H]
                    sp.dma_start(wfr[:, :, H * e:H * (e + 1)], src.rearrange("l p k n -> p (l k) n")).then_inc(wf_loaded, 16)
                ffn("ffn1", L)
                fv = S["fv"]
                for k in range(2):
                    load(fv, k, L, 0, ("w_in", 0, KD, COL_V + 256 * k, 256))
                mn = S["mixnorm"]
                wait_apart(sp, filled[mn.slot(0)], mn.turn(0, L) + 1)
                for s in range(SB):
                    for g in range(NPG):
                        page = sp.value_load(pages[0:1, s * NPG + g:s * NPG + g + 1], min_val=0, max_val=t_in["cache_k"].shape[0] - 1)
                        src = t_in["cache_logf"][bass.ds(page, 1), bass.ds(L, 1), :, :].rearrange("a b t h -> (a b t) h")
                        sp.dma_start(lfp[:, g, s * H:(s + 1) * H], src).then_inc(lfp_loaded, 16)
                pr = S["pair"]
                with sp.Fori(0, PAIRS) as p:
                    def pages_of(name):
                        for s in range(SB):
                            for g in range(NPG):
                                page = sp.value_load(pages[0:1, s * NPG + g:s * NPG + g + 1], min_val=0, max_val=t_in["cache_k"].shape[0] - 1)
                                src = t_in[name].rearrange("a l t h d -> a l t (h d)")[bass.ds(page, 1), bass.ds(L, 1), :, bass.ds(p * P, P)]
                                sp.dma_start(kv[:, s * NPG + g, :], src.rearrange("a b t n -> (a b t) n")).then_inc(kv_loaded, 16)

                    load(pr, 0, L, p, ("w_in", 0, KD, p * P + COL_Q, P), ("w_in", 0, KD, p * P + COL_K, P))
                    load(pr, 1, L, p, ("w_in", 0, KD, p * P + COL_BX, P), ("w_in", 0, KD, p * P + COL_BY, P))
                    wait_apart(sp, filled[pr.slot(20)], pr.turn(20, L, p) - 5)
                    pages_of("cache_k")
                    load(pr, 2, L, p, ("w_in", 0, KD, p * P + COL_SC, P), ("w_in", 0, KD, p * P + COL_SX, P))
                    wait_apart(sp, filled[pr.slot(3)], pr.turn(3, L, p) + 1)
                    pages_of("cache_v")
                    load(pr, 3, L, p, ("w_in", 0, KD, p * P + COL_SB, P))
                    sp.wait_ge(filled[pr.slot(12)], pr.turn(12, L, p) + 1)
                    for j, name in enumerate(("lru_wa", "lru_wx")):
                        for e in range(2):
                            src = t_in[name][bass.ds(L, 1), bass.ds(p * 2 + e, 1), :, :].rearrange("a b i j -> (a b i) j")
                            sp.dma_start(wab[HD * e:HD * (e + 1), j, HD * e:HD * (e + 1)], src).then_inc(wab_loaded, 16)
                mg = S["merge"]
                with sp.Fori(0, mg.steps) as i:
                    for b in range(3):
                        load(mg, 2 * b, L, i, ("w_in", 0, KD, i * 256 + (COL_G + D * b), 256))
                        load(mg, 2 * b + 1, L, i, ("w_branch", 4 * b, 4, i * 256, 256))
                with sp.Fori(0, 2) as i:
                    for k in range(2):
                        load(S["out"], k, L, i, ("w_out", 0, KD, i * 512 + 256 * k, 256))
                ffn("ffn2", L)
            sp.wait_ge(lo_ready, 2 * DEPTH * plan["layer_units"] - 2 + AHEAD)
            src = t_in["w_out"].rearrange("l (k p) n -> l p k n", p=P)[0, :, :, 0:256]
            sp.dma_start(wraw[:, 0, :].rearrange("p (k c) -> p k c", c=256), src).then_inc(unit_loaded[0], 32)
            post = DEPTH * plan["layer_tiles"] + PRE_TILES
            for b in range(5):
                sp.wait_ge(freed[(post + b) % 4], (post + b) // 4 + 1)
                if b < 4:
                    sp.dma_start(t_out["y_prompt"][0, b * P:(b + 1) * P, :], yout[:, b, :]).then_inc(y_stored, 16)
                else:
                    sp.dma_start(t_out["y_sample"].rearrange("s t d -> (s t) d"), yout[NS:P, b, :]).then_inc(y_stored, 16)
            sp.wait_ge(y_stored, 5 * 16)
            sp.wait_ge(v_stored, DEPTH * 32)
            sp.wait_ge(k_stored, DEPTH * PAIRS * 32)
            sp.wait_ge(lf_stored, DEPTH * 32)
            sp.wait_ge(f_stored, DEPTH * 96)

        @block.tensor
        def _(pe):
            def wait_psum(st, k, L, i=0):
                pe.wait_ge(freed[st.slot(k)], st.turn(k, L, i))

            def wait_weights(st, w, L, i=0):
                pe.wait_ge(lo_ready, st.unit(0, L, i) * 2 + (w + 1 + AHEAD))

            def project(slot, w, chunks, rhs_hi, rhs_lo, start=True, stop=True):
                for c, k in enumerate(chunks):
                    for half in range(2):
                        span = slice(half * HF, half * HF + HF)
                        out = ps[slot][:, half, 0:HF]
                        wh, wl = whi[:, w % 2, c * P:(c + 1) * P], wlo[:, w % 2, c * P:(c + 1) * P]
                        pe.matmul(out, wh, rhs_hi[:, k, span], start=(start and c == 0), stop=False)
                        pe.matmul(out, wh, rhs_lo[:, k, span], start=False, stop=False)
                        last = pe.matmul(out, wl, rhs_hi[:, k, span], start=False, stop=(stop and c == len(chunks) - 1))
                return last

            def plain(st, k, w, chunks, rhs_hi, rhs_lo, L, i=0):
                wait_weights(st, w, L, i)
                wait_psum(st, k, L, i)
                project(st.slot(k), w, chunks, rhs_hi, rhs_lo).then_inc(filled[st.slot(k)], 1)

            def norm(st, n, L):
                pe.wait_ge(sq_added, L * 24 + 8 * (n + 1))
                wait_psum(st, 0, L)
                for half in range(2):
                    last = pe.matmul(ps[st.slot(0)][:, half, 0:HF], ones, tmp[6][:, half * HF:half * HF + HF],
                                     start=True, stop=True)
                last.then_inc(filled[st.slot(0)], 1)

            def ffn(name, n, L):
                norm(S[name + "norm"], n, L)
                wait_apart(pe, h_ready, L * 24 + 8 * (n + 1))
                done = 0
                for st_in, st_out, kc in S[name]:
                    with pe.Fori(0, st_in.steps) as i:
                        for k in range(4):
                            plain(st_in, k, k, range(KD), hh, hl, L, i)
                    done += kc
                    wait_apart(pe, a_ready, L * 44 + (22 * (n // 2) + done))
                    with pe.Fori(0, 2) as i:
                        for k in range(4):
                            plain(st_out, k, k, range(kc), ah, al, L, i)

            pe.wait_ge(consts_ready, 1)
            for c in range(KD):
                if c >= 4:
                    pe.wait_ge(freed[c % 4], c // 4)
                for b in range(5):
                    rows_ = P if b < 4 else NS
                    out = ps[c % 4][:, 0, b * P:(b + 1) * P] if b < 4 else ps[c % 4][:, 1, 0:NS]
                    last = pe.transpose(out, xin[0:rows_, b, c * P:(c + 1) * P], ident[0:rows_, 0:rows_])
                last.then_inc(filled[c % 4], 1)
            for g in (8, 9):
                pe.wait_ge(freed[g % 4], g // 4)
                for l in range(DEPTH):
                    if g == 8:
                        for t in range(4):
                            last = pe.transpose(ps[0][:, l, t * NR:(t + 1) * NR], rows[:, l, t * P:(t + 1) * P], ident[0:NR, 0:NR])
                    else:
                        last = pe.transpose(ps[1][:, 0, l * 26:(l + 1) * 26], rowsg[:, l, :], ident[0:26, 0:26])
                last.then_inc(filled[g % 4], 1)
            for g in (10, 11):
                pe.wait_ge(freed[g % 4], g // 4)
                pe.transpose(ps[g % 4][:, 0, 0:P], ident, ident).then_inc(filled[g % 4], 1)

            with pe.Fori(0, DEPTH) as L:
                ffn("ffn1", 0, L)
                norm(S["mixnorm"], 1, L)

                fv = S["fv"]
                pe.wait_ge(h_ready, L * 24 + 16)
                pe.wait_ge(wf_ready, L + 2)
                wait_psum(fv, 0, L)
                for k in range(KD):
                    for half in range(2):
                        span = slice(half * HF, half * HF + HF)
                        out = ps[fv.slot(0)][:, half, 0:HF]
                        wh, wl = wfh[:, k * F_W:k * F_W + P], wfl[:, k * F_W:k * F_W + P]
                        pe.matmul(out, wh, hh[:, k, span], start=(k == 0), stop=False)
                        pe.matmul(out, wh, hl[:, k, span], start=False, stop=False)
                        last = pe.matmul(out, wl, hh[:, k, span], start=False, stop=(k == KD - 1))
                last.then_inc(filled[fv.slot(0)], 1)
                pe.wait_ge(lfp_ready, L + 1)
                wait_psum(fv, 1, L)
                for g in range(NPG):
                    last = pe.transpose(ps[fv.slot(1)][:, 0, g * P:(g + 1) * P], lfp[:, g, :], ident)
                last.then_inc(filled[fv.slot(1)], 1)

                def values(u):
                    wait_weights(fv, 2 * u + 1, L)
                    for b in range(5):
                        k_ = (2, 5)[u] + (b == 4)
                        if b in (0, 4):
                            wait_psum(fv, k_, L)
                        out = ps[fv.slot(k_)][:, b // 2 % 2, (b % 2) * 256:(b % 2) * 256 + 256]
                        tok = slice(b * P, b * P + P) if b < 4 else slice(N - P, N)
                        for k in range(KD):
                            rh = whi[:, :, k * P:(k + 1) * P]
                            rl = wlo[:, :, k * P:(k + 1) * P]
                            pe.matmul(out, hh[:, k, tok], rh, start=(k == 0), stop=False)
                            pe.matmul(out, hl[:, k, tok], rh, start=False, stop=False)
                            last = pe.matmul(out, hh[:, k, tok], rl, start=False, stop=(k == KD - 1))
                        if b in (3, 4):
                            last.then_inc(filled[fv.slot(k_)], 1)

                values(0)
                pe.wait_ge(logf_ready, L + 1)
                wait_psum(fv, 4, L)
                pe.matmul(ps[fv.slot(4)][:, 0, 0:NS], const[0:H, C_REP:C_REP + P], lf[0:H, SEQ:N], start=True, stop=True)\
                    .then_inc(filled[fv.slot(4)], 1)
                values(1)
                wait_apart(pe, freed[fv.slot(7)], fv.turn(7, L))
                for b in range(5):
                    tok = slice(b * P, b * P + P) if b < 4 else slice(N - P, N)
                    last = pe.transpose(ps[fv.slot(7)][:, 0, b * H:(b + 1) * H], lf[0:H, tok], ident[0:H, 0:H])
                last.then_inc(filled[fv.slot(7)], 1)

                pr = S["pair"]
                with pe.Fori(0, PAIRS) as p:
                    it = L * PAIRS + p
                    plain(pr, 0, 0, range(KD), hh, hl, L, p)
                    plain(pr, 1, 1, range(KD), hh, hl, L, p)
                    pe.wait_ge(kv_loaded, it * 512 + 256)
                    for k in (2, 3):
                        wait_psum(pr, k, L, p)
                        for g in range(8):
                            last = pe.transpose(ps[pr.slot(k)][:, g // 4, (g % 4) * P:(g % 4 + 1) * P], kv[:, (k - 2) * 8 + g, :], ident)
                        last.then_inc(filled[pr.slot(k)], 1)
                    for k in (4, 5):
                        pe.wait_ge(qk_squared, it * 2 + (k - 3))
                        wait_psum(pr, k, L, p)
                        for half in range(2):
                            last = pe.matmul(ps[pr.slot(k)][:, half, 0:HF], bones, tmp[k - 4][:, half * HF:half * HF + HF], start=True, stop=True)
                        last.then_inc(filled[pr.slot(k)], 1)
                    plain(pr, 6, 2, range(KD), hh, hl, L, p)
                    plain(pr, 7, 3, range(KD), hh, hl, L, p)
                    pe.wait_ge(qk_ready, it + 1)
                    for e in range(2):
                        for qb in range(QB):
                            k = 8 + 2 * e + qb // 2
                            if qb % 2 == 0:
                                wait_psum(pr, k, L, p)
                            n = (qb + 1) * P
                            out = ps[pr.slot(k)][:, qb % 2, :]
                            hs = slice(HD * e, HD * (e + 1))
                            qs = slice(qb * P, (qb + 1) * P)
                            pe.matmul(out[:, 0:n], qp[hs, qs], kp[hs, 0:n], start=True, stop=False)
                            pe.matmul(out[:, 0:n], cq[e][:, qs], ck[:, 0:n], start=False, stop=False)
                            last = pe.matmul(out[:, qb * P:n], identb[:], maskd[:], start=False, stop=True)
                            if qb % 2:
                                last.then_inc(filled[pr.slot(k)], 1)
                    wait_psum(pr, 12, L, p)
                    for k in (2, 3):
                        pe.wait_ge(freed[pr.slot(k)], pr.turn(k, L, p) + 1)
                    out = ps[pr.slot(12)][:, 0, :]
                    pe.matmul(out[:, 0:3 * P], lhss[:], rhss[:], start=True, stop=False, skip_group_check=True)
                    pe.matmul(out[:, PAST:PAST + P], identb[:], masks[:], start=False, stop=False, skip_group_check=True)
                    for q in qeo:
                        pe.matmul(out[:, PAST:PAST + P], q[:], kp[:, N - P:N], start=False, stop=False, skip_group_check=True)
                    for s in range(SB):
                        quad = slice(32 * (s // 2), 32 * (s // 2) + 32)
                        pe.matmul(out[quad, 0:PAST], qeo[s % 2][:, quad], kpt[:, s * PAST:(s + 1) * PAST],
                                  start=False, stop=(s == SB - 1), skip_group_check=True, tile_position=(0, quad.start))
                    pe.transpose(ps[pr.slot(12)][:, 0, 3 * P:4 * P], kp[:, N - P:N], ident)
                    for b in range(4):
                        last = pe.transpose(ps[pr.slot(12)][:, 1, b * P:(b + 1) * P], kp[:, b * P:(b + 1) * P], ident)
                    last.then_inc(filled[pr.slot(12)], 1)
                    plain(pr, 13, 4, range(KD), hh, hl, L, p)
                    plain(pr, 14, 5, range(KD), hh, hl, L, p)
                    pe.wait_ge(xc_ready, it + 1)
                    pe.wait_ge(wab_loaded, it * 64 + 64)
                    for k in (15, 16):
                        wait_psum(pr, k, L, p)
                        for half in range(2):
                            last = pe.matmul(ps[pr.slot(k)][:, half, 0:XB // 2], wab[:, k - 15, :],
                                             tmp[3][:, half * (XB // 2):(half + 1) * (XB // 2)], start=True, stop=True)
                        last.then_inc(filled[pr.slot(k)], 1)

                    offs = [0, P, 3 * P, 6 * P]
                    koffs = [0, 4 * P, 7 * P, 9 * P]

                    def transposed(e, k0):
                        pe.wait_ge(prob_ready, it * 3 + (e + 1))
                        for kb in range(QB):
                            k = k0 + kb // 2
                            if kb % 2 == 0:
                                wait_psum(pr, k, L, p)
                            for qb in range(kb, QB):
                                last = pe.transpose(ps[pr.slot(k)][:, kb % 2, (qb - kb) * P:(qb - kb + 1) * P],
                                                    prob[e][:, offs[qb] + kb * P:offs[qb] + (kb + 1) * P], ident)
                            if kb % 2:
                                last.then_inc(filled[pr.slot(k)], 1)

                    def weighted(e):
                        k = 18 + 4 * e
                        pe.wait_ge(freed[pr.slot(k)], pr.turn(k, L, p) + 1)
                        for kb in range(QB):
                            last = pe.matmul(ps[pr.slot(20)][HD * e:HD * (e + 1), 0, kb * P:SEQ], vp[:, kb, HD * e:HD * (e + 1)],
                                             probt[:, koffs[kb]:koffs[kb] + (QB - kb) * P], start=(kb == 0), stop=(kb == QB - 1),
                                             skip_group_check=True)
                        if e == 0:
                            last.then_inc(pv_done, 1)

                    transposed(0, 17)
                    wait_weights(pr, 6, L, p)
                    wait_psum(pr, 19, L, p)
                    project(pr.slot(19), 6, range(4), hh, hl, stop=False)
                    wait_weights(pr, 7, L, p)
                    project(pr.slot(19), 7, range(4, KD), hh, hl, start=False).then_inc(filled[pr.slot(19)], 1)
                    pe.wait_ge(vp_ready, it + 1)
                    wait_psum(pr, 20, L, p)
                    weighted(0)
                    transposed(1, 21)
                    pe.wait_ge(prob_ready, it * 3 + 3)
                    wait_psum(pr, 23, L, p)
                    for c in range(3):
                        last = pe.transpose(ps[pr.slot(23)][:, 0, c * P:(c + 1) * P], probs[:, c * P:(c + 1) * P], ident)
                    last.then_inc(filled[pr.slot(23)], 1)
                    weighted(1)
                    pe.wait_ge(freed[pr.slot(23)], pr.turn(23, L, p) + 1)
                    pe.wait_ge(kv_loaded, it * 512 + 512)
                    out = ps[pr.slot(20)][:, 1, :]
                    pe.matmul(out[:, 0:P], vp[:, 4, :], probst[:, 2 * P:3 * P], start=True, stop=False, skip_group_check=True)
                    for s in range(SB):
                        rs = slice(16 * s, 16 * s + 16)
                        for g in range(NPG):
                            last = pe.matmul(out[:, rs], kv[:, s * NPG + g, :], probst[:, g * P + 16 * s:g * P + 16 * s + 16],
                                             start=False, stop=(s == SB - 1 and g == NPG - 1), skip_group_check=True)
                    last.then_inc(filled[pr.slot(20)], 1)

                st = S["state"]
                pe.wait_ge(f_ready, L + 1)
                wait_apart(pe, freed[st.slot(0)], st.turn(0, L))
                for t in range(4):
                    last = pe.transpose(ps[st.slot(0)][0:NO, 0, t * P:(t + 1) * P], fout[:, t, :], ident)
                last.then_inc(filled[st.slot(0)], 1)

                mg = S["merge"]
                with pe.Fori(0, mg.steps) as i:
                    for b in range(3):
                        for j in range(2):
                            plain(mg, 4 * b + j, 4 * b + j, range(KD), hh, hl, L, i)
                        pe.wait_ge(o_ready, L * 12 + 4 * (b + 1))
                        for j in range(2, 4):
                            plain(mg, 4 * b + j, 4 * b + j, range(4 * b, 4 * b + 4), oh, ol, L, i)
                wait_apart(pe, m_ready, L * 8 + 8)
                with pe.Fori(0, 2) as i:
                    for k in range(4):
                        plain(S["out"], k, k, range(KD), hh, hl, L, i)
                ffn("ffn2", 2, L)
                for g in range(plan["tiles_used"], plan["layer_tiles"]):
                    pe.wait_ge(freed[g % 4], L * (plan["layer_tiles"] // 4) + (PRE_TILES + g) // 4)
                    pe.transpose(ps[g % 4][:, 0, 0:P], ident, ident).then_inc(filled[g % 4], 1)

            post = DEPTH * plan["layer_tiles"] + PRE_TILES
            last_st = S["ffn2"][-1][1]
            for k in range(4):
                pe.wait_ge(freed[last_st.slot(k)], last_st.turn(k, DEPTH - 1, 1) + 1)
            for b in range(5):
                g = post + b
                tok = slice(b * P, b * P + P) if b < 4 else slice(N - P, N)
                pe.wait_ge(freed[g % 4], g // 4)
                for c in range(KD):
                    last = pe.transpose(ps[g % 4][:, c // 4, (c % 4) * P:(c % 4 + 1) * P], x[:, c, tok], ident)
                last.then_inc(filled[g % 4], 1)

        @block.scalar
        def _(act):
            def wait_tile(st, k, L, i=0):
                act.wait_ge(filled[st.slot(k)], st.turn(k, L, i) + 1)

            def split_ahead(st, w, k, L, i=0):
                wait_tile(st, k, L, i)
                u, j, rowwise = ahead(st, w)
                base = st.first_unit + u
                slot = base % 2
                act.wait_ge(unit_loaded[slot], L * (plan["layer_units"] // 2 * 32) + i * (st.units // 2 * 32) + (base // 2 + 1) * 32)
                act.activation(split_tile(whi, j, rowwise), raw_tile(slot, j, rowwise), ACT.Copy).then_inc(hi_ready, 1)

            def norm(st, n, L):
                wait_tile(st, 0, L)
                act.activation(two(tmp[5][:, 0:N]), cols(st.slot(0)), ACT.Sqrt, bias=eps[:, 0:1]).then_inc(freed[st.slot(0)], 1)
                for c in range(KD):
                    act.wait_ge(hf_ready, L * 24 + (8 * n + c + 1))
                    act.activation(hh[:, c, :], tmp[c % 2][:, 0:N], ACT.Copy).then_inc(hh_ready, 1)

            def out_squares(st, q0, L):
                with act.Fori(0, 2) as i:
                    for k in range(4):
                        split_ahead(st, k, k, L, i)
                        if q0 is None:
                            continue
                        act.wait_ge(freed[st.slot(k)], st.turn(k, L, i) + 1)
                        act.wait_ge(sq_added, L * 24 + i * 4 + (q0 + k - 1))
                        xm = x[:, bass.ds(i * 4 + k, 1), :].rearrange("p a n -> p (a n)")
                        act.activation(tmp[2 + k % 2][:, 0:N], xm, ACT.Square).then_inc(sq_ready, 1)

            def ffn(name, n, L):
                norm(S[name + "norm"], n, L)
                for part, (st_in, st_out, kc) in enumerate(S[name]):
                    with act.Fori(0, st_in.steps) as i:
                        for k in range(4):
                            split_ahead(st_in, k, k, L, i)
                            if k < 2:
                                act.wait_ge(freed[st_in.slot(k + 2)], st_in.turn(k + 2, L, i))
                                act.activation(two(tmp[k][:, 0:N]), cols(st_in.slot(k)), ACT.Silu).then_inc(freed[st_in.slot(k)], 1)
                    out_squares(st_out, 8 * (n + 1) if part == 2 else None, L)

            act.wait_ge(pre_done, 1)
            for c in range(KD):
                act.wait_ge(filled[c % 4], c // 4 + 1)
                act.activation(x[:, c, 0:SEQ], ps[c % 4][:, 0, :], ACT.Copy)
                act.activation(x[:, c, SEQ:N], ps[c % 4][:, 1, 0:NS], ACT.Copy).then_inc(freed[c % 4], 1)
            act.wait_ge(filled[0], 3)
            act.activation(par_all[:, :, :], ps[0][:, :, 0:4 * NR], ACT.Copy).then_inc(freed[0], 1)
            act.wait_ge(filled[1], 3)
            act.activation(gains[:, :, :].rearrange("p l n -> p (l n)"), ps[1][:, 0, 0:52], ACT.Copy).then_inc(freed[1], 1)
            for g in (10, 11):
                act.wait_ge(filled[g % 4], g // 4 + 1)
                act.activation(small[:, 60:61], ps[g % 4][:, 0, 0:1], ACT.Copy).then_inc(freed[g % 4], 1)
                act.drain()
            act.drain()
            for c in range(KD):
                if c >= 2:
                    act.wait_ge(sq_added, c - 1)
                act.activation(tmp[2 + c % 2][:, 0:N], x[:, c, :], ACT.Square).then_inc(sq_ready, 1)
            act.wait_ge(pre_done, 2)
            act.activation(spt[1][:], spt[0][:], ACT.Exp, scale=-1.0).then_inc(consts_ready, 1)
            for j in range(2):
                act.wait_ge(unit_loaded[0], 32)
                act.activation(split_tile(whi, j), raw_tile(0, j), ACT.Copy).then_inc(hi_ready, 1)

            with act.Fori(0, DEPTH) as L:
                act.wait_ge(wf_loaded, L * 32 + 32)
                act.activation(wfh[:, 0:KD * F_W], wfr[:, :, :].rearrange("p k c -> p (k c)"), ACT.Copy).then_inc(wf_hi, 1)
                ffn("ffn1", 0, L)
                norm(S["mixnorm"], 1, L)
                fv = S["fv"]
                act.wait_ge(absz_ready, L + 1)
                act.activation(tmp[3][0:F_W, 0:N], tmp[2][0:F_W, 0:N], ACT.Exp, scale=-1.0).then_inc(expz_ready, 1)
                wait_tile(fv, 1, L)
                act.activation(cs[:, 0:PAST], ps[fv.slot(1)][:, 0, 0:PAST], ACT.Copy).then_inc(freed[fv.slot(1)], 1)
                for u in range(2):
                    wait_tile(fv, (2, 5)[u], L)
                    act.activation(vtok[:, 0:4, u * 256:(u + 1) * 256],
                                   ps[fv.slot((2, 5)[u])][:, :, :].rearrange("p b (c n) -> p (b c) n", n=256), ACT.Copy)\
                        .then_inc(freed[fv.slot((2, 5)[u])], 1)
                    split_ahead(fv, 2 * u, (3, 6)[u], L)
                    split_ahead(fv, 2 * u + 1, (3, 6)[u], L)
                    act.activation(vtok[:, 4, u * 256:(u + 1) * 256], ps[fv.slot((3, 6)[u])][:, 0, 0:256], ACT.Copy)\
                        .then_inc(freed[fv.slot((3, 6)[u])], 1)
                wait_tile(fv, 7, L)
                act.activation(lfo[:, :, :].rearrange("p b h -> p (b h)"), ps[fv.slot(7)][:, 0, 0:5 * H], ACT.Copy)\
                    .then_inc(freed[fv.slot(7)], 1)

                pr = S["pair"]
                with act.Fori(0, PAIRS) as p:
                    it = L * PAIRS + p

                    def free(k):
                        return freed[pr.slot(k)]

                    for k in (0, 1):
                        split_ahead(pr, k, k, L, p)
                        act.activation(two(tmp[k][:, 0:N]), cols(pr.slot(k)), ACT.Square).then_inc(qk_squared, 1)
                        act.activation(two((qp, kp)[k][:]), cols(pr.slot(k)), ACT.Copy).then_inc(free(k), 1)
                    for k in (2, 3):
                        wait_tile(pr, k, L, p)
                        act.activation(kpt[:, (k - 2) * 1024:(k - 1) * 1024], ps[pr.slot(k)][:, :, :].rearrange("p b n -> p (b n)"), ACT.Copy)\
                            .then_inc(free(k), 1)
                    for k in (4, 5):
                        wait_tile(pr, k, L, p)
                        act.activation(two(tmp[k - 4][:, 0:N]), cols(pr.slot(k)), ACT.Sqrt, bias=eps[:, 0:1]).then_inc(free(k), 1)
                    split_ahead(pr, 2, 6, L, p)
                    bx = ps[pr.slot(6)]
                    act.activation(tmp[2][:, HB_:HB_ + HF], bx[:, 0, 0:HF], ACT.Copy)
                    act.activation(tmp[2][:, HB_ + HF:HB_ + SEQ], bx[:, 1, 0:SEQ - HF], ACT.Copy)
                    smp = sequences(tmp[2], SB0, STEP_B, HB_, ST)
                    act.activation(smp, bx[:, 1, SEQ - HF:HF].rearrange("p (s t) -> p s t", t=ST), ACT.Copy).then_inc(free(6), 1)
                    split_ahead(pr, 3, 7, L, p)
                    gp = o[:, bass.ds(p + 4, 1), :].rearrange("p a (b n) -> p (a b) n", b=2)
                    act.activation(gp, cols(pr.slot(7)), ACT.Gelu_apprx_tanh).then_inc(free(7), 1)

                    for e in range(2):
                        act.wait_ge(max_ready, it * 3 + (e + 1))
                        for qb in range(QB):
                            k = 8 + 2 * e + qb // 2
                            n = (qb + 1) * P
                            off = (0, P, 3 * P, 6 * P)[qb]
                            ins = act.activation(prob[e][:, off:off + n], ps[pr.slot(k)][:, qb % 2, 0:n], ACT.Exp,
                                                 bias=small[:, 4 * e + qb:4 * e + qb + 1], accum_out=small[:, 16 + 4 * e + qb:17 + 4 * e + qb])
                            if qb % 2:
                                ins.then_inc(free(k), 1)
                    act.wait_ge(max_ready, it * 3 + 3)
                    act.activation(probs[:], ps[pr.slot(12)][:, 0, 0:3 * P], ACT.Exp, bias=small[:, 8:9], accum_out=small[:, 24:25])\
                        .then_inc(exp_ready, 1)
                    act.activation(kout[:, 4, :], ps[pr.slot(12)][:, 0, 3 * P:4 * P], ACT.Copy)
                    act.activation(kout[:, 0:4, :].rearrange("p b n -> p (b n)"), ps[pr.slot(12)][:, 1, :], ACT.Copy).then_inc(free(12), 1)
                    split_ahead(pr, 4, 13, L, p)
                    act.activation(two(tmp[5][:, 0:N]), cols(pr.slot(13)), ACT.Copy).then_inc(free(13), 1)
                    split_ahead(pr, 5, 14, L, p)
                    for k in (15, 16):
                        wait_tile(pr, k, L, p)
                        act.activation(tmp[(4, 1)[k - 15]][:, 0:XB].rearrange("p (b n) -> p b n", b=2), ps[pr.slot(k)][:, :, 0:XB // 2],
                                       ACT.Sigmoid, bias=prow[:, R_BA + (k - 15):R_BA + 1 + (k - 15)]).then_inc(free(k), 1)
                    act.wait_ge(free(16), pr.turn(16, L, p) + 1)
                    act.wait_ge(free(14), pr.turn(14, L, p) + 1)
                    act.activation(tmp[0][:, 0:XB], tmp[4][:, 0:XB], ACT.Exp, scale=nbias[:, 0:1])
                    act.activation(tmp[5][:, 0:XB], tmp[4][:, 0:XB], ACT.Tanh, scale=nbias[:, 1:2])
                    act.drain()
                    act.activation(tmp[4][:, 0:XB], tmp[0][:, 0:XB], ACT.Square).then_inc(gates_ready, 1)

                    def copy_pt(k0):
                        for kb in range(QB):
                            k = k0 + kb // 2
                            if kb % 2 == 0:
                                wait_tile(pr, k, L, p)
                            w = (QB - kb) * P
                            off = (0, 4 * P, 7 * P, 9 * P)[kb]
                            ins = act.activation(probt[:, off:off + w], ps[pr.slot(k)][:, kb % 2, 0:w], ACT.Copy)
                            if kb == 1:
                                ins.then_inc(free(k), 1)
                        ins.then_inc(free(k0 + 1), 1)

                    copy_pt(17)
                    act.wait_ge(root_in, it + 1)
                    act.activation(tmp[5][:, 0:XB], tmp[5][:, 0:XB], ACT.Sqrt, bias=eps[:, 1:2]).then_inc(root_ready, 1)
                    split_ahead(pr, 6, 19, L, p)
                    split_ahead(pr, 7, 19, L, p)
                    act.wait_ge(pv_done, it + 1)
                    copy_pt(21)
                    wait_tile(pr, 23, L, p)
                    act.activation(probst[:], ps[pr.slot(23)][:, 0, 0:3 * P], ACT.Copy).then_inc(free(23), 1)
                    wait_tile(pr, 20, L, p)
                    op = o[:, bass.ds(p, 1), :].rearrange("p a n -> p (a n)")
                    act.activation(op[:, 0:SEQ], ps[pr.slot(20)][:, 0, :], ACT.Copy)
                    for e in range(2):
                        hs = slice(HD * e, HD * (e + 1))
                        src = ps[pr.slot(20)][hs, 1, 0:P].rearrange("p (s c) -> p s c", c=16)[:, :, ST * e:ST * (e + 1)]
                        dst = o[hs, bass.ds(p, 1), SEQ:N].rearrange("p a (s t) -> p (a s) t", t=ST)
                        ins = act.activation(dst, src, ACT.Copy)
                    ins.then_inc(free(20), 1)
                    act.wait_ge(k_stored, it * 32 + 32)

                st = S["state"]
                wait_tile(st, 0, L)
                act.wait_ge(f_ready, L + 1)
                for c in range(12):
                    act.activation(oh[:, c, :], o[:, c, :], ACT.Copy).then_inc(oh_ready, 1)
                act.activation(frow[:, :], ps[st.slot(0)][0:NO, 0, :], ACT.Copy).then_inc(freed[st.slot(0)], 1)
                mg = S["merge"]
                with act.Fori(0, mg.steps) as i:
                    for b in range(3):
                        for j in range(4):
                            k = 4 * b + j
                            split_ahead(mg, k, k, L, i)
                            if j < 2:
                                if b:
                                    act.wait_ge(freed[mg.slot(k - 2)], mg.turn(k - 2, L, i) + 1)
                                else:
                                    act.wait_ge(freed[mg.slot(k + 10)], mg.turn(k + 10, L, i) - 2)
                                act.activation(two(tmp[j][:, 0:N]), cols(mg.slot(k)), ACT.Sigmoid).then_inc(freed[mg.slot(k)], 1)
                act.wait_ge(merged_ready, L + 1)
                for c in range(KD):
                    act.activation(hh[:, c, :], merged[:, c, :], ACT.Copy).then_inc(mh_ready, 1)
                out_squares(S["out"], 16, L)
                ffn("ffn2", 2, L)
                act.wait_ge(v_stored, L * 32 + 32)
                act.wait_ge(lf_stored, L * 32 + 32)
                act.wait_ge(f_stored, L * 96 + 96)
                for g in range(plan["tiles_used"], plan["layer_tiles"]):
                    act.wait_ge(filled[g % 4], L * (plan["layer_tiles"] // 4) + (PRE_TILES + g) // 4 + 1)
                    act.activation(small[:, 60:61], ps[g % 4][:, 0, 0:1], ACT.Copy).then_inc(freed[g % 4], 1)
                    act.drain()

            post = DEPTH * plan["layer_tiles"] + PRE_TILES
            for b in range(5):
                g = post + b
                act.wait_ge(filled[g % 4], g // 4 + 1)
                act.activation(yout[:, b, :], ps[g % 4][:, :, :].rearrange("p b n -> p (b n)"), ACT.Copy).then_inc(freed[g % 4], 1)

        @block.vector
        def _(dve):
            def wait_tile(st, k, L, i=0):
                dve.wait_ge(filled[st.slot(k)], st.turn(k, L, i) + 1)

            def split_ahead(st, w, L, i=0):
                u, j, rowwise = ahead(st, w)
                slot = (st.first_unit + u) % 2
                dve.wait_ge(hi_ready, st.unit(0, L, i) * 2 + (w + 3))
                dve.tensor_tensor(split_tile(wlo, j, rowwise), raw_tile(slot, j, rowwise), split_tile(whi, j, rowwise).bitcast(F32),
                                  ALU.subtract).then_inc(lo_ready, 1)

            def norm(st, n, L):
                dve.wait_ge(freed[st.slot(0)], st.turn(0, L) + 1)
                dve.reciprocal(tmp[4][:, 0:N], tmp[5][:, 0:N])
                dve.drain()

                def scaled(c):
                    dve.scalar_tensor_tensor(out=tmp[c % 2][:, 0:N], in0=x[:, c, :], scalar=gain[:, 8 * n + c:8 * n + c + 1],
                                             in1=tmp[4][:, 0:N], op0=ALU.mult, op1=ALU.mult).then_inc(hf_ready, 1)

                scaled(0)
                for c in range(KD):
                    if c + 1 < KD:
                        dve.drain()
                        scaled(c + 1)
                    dve.wait_ge(hh_ready, L * 24 + (8 * n + c + 1))
                    dve.tensor_tensor(hl[:, c, :], tmp[c % 2][:, 0:N], hh[:, c, :].bitcast(F32), ALU.subtract).then_inc(h_ready, 1)

            def update(st, L, half):
                with dve.Fori(0, 2) as i:
                    for k in range(4):
                        split_ahead(st, k, L, i)
                        wait_tile(st, k, L, i)
                        xm = x[:, bass.ds(i * 4 + k, 1), :].rearrange("p a (b n) -> p (a b) n", b=2)
                        dve.scalar_tensor_tensor(out=xm, in0=cols(st.slot(k)), scalar=half, in1=xm, op0=ALU.mult, op1=ALU.add)\
                            .then_inc(freed[st.slot(k)], 1)

            def ffn(name, n, L):
                norm(S[name + "norm"], n, L)
                for st_in, st_out, kc in S[name]:
                    with dve.Fori(0, st_in.steps) as i:
                        for k in range(4):
                            split_ahead(st_in, k, L, i)
                            if k < 2:
                                continue
                            wait_tile(st_in, k, L, i)
                            dve.wait_ge(freed[st_in.slot(k - 2)], st_in.turn(k - 2, L, i) + 1)
                            pf = tmp[2 + k]
                            dve.tensor_tensor(two(pf[:, 0:N]), two(tmp[k - 2][:, 0:N]), cols(st_in.slot(k)), ALU.mult)\
                                .then_inc(freed[st_in.slot(k)], 1)
                            dve.drain()
                            j = i * 2 + (k - 2)
                            ahj = ah[:, bass.ds(j, 1), :].rearrange("p a n -> p (a n)")
                            alj = al[:, bass.ds(j, 1), :].rearrange("p a n -> p (a n)")
                            dve.tensor_copy(ahj, pf[:, 0:N])
                            dve.drain()
                            dve.tensor_tensor(alj, pf[:, 0:N], ahj.bitcast(F32), ALU.subtract).then_inc(a_ready, 1)
                    update(st_out, L, 0.5)

            def log1p(t, r, s, s2, acc):
                dve.tensor_scalar(r, t, 2.0, None, ALU.add)
                dve.drain()
                dve.reciprocal(r, r)
                dve.drain()
                dve.tensor_tensor(s, t, r, ALU.mult)
                dve.drain()
                dve.tensor_tensor(s2, s, s, ALU.mult)
                dve.drain()
                dve.tensor_scalar(acc, s2, 1.0 / 17, None, ALU.mult)
                for k in range(15, 1, -2):
                    dve.drain()
                    dve.scalar_tensor_tensor(out=acc, in0=acc, scalar=1.0 / k, in1=s2, op0=ALU.add, op1=ALU.mult)
                dve.drain()
                dve.scalar_tensor_tensor(out=acc, in0=acc, scalar=1.0, in1=s, op0=ALU.add, op1=ALU.mult)
                dve.drain()
                dve.tensor_scalar(acc, acc, 2.0, None, ALU.mult)
                dve.drain()

            dve.memset(eps[:, 0:1], EPS)
            dve.memset(eps[:, 1:2], 2e-35)
            dve.memset(wfh[:, KD * F_W:].bitcast(F32), 0.0)
            dve.memset(wfl[:, KD * F_W:].bitcast(F32), 0.0)
            dve.memset(wab[:, :, :], 0.0)
            dve.memset(small[:], 0.0).then_inc(pre_done, 1)
            dve.memset(wlo[:, 0, 0:1].bitcast(F32), 0.0).then_inc(lo_ready, AHEAD)
            dve.memset(wlo[:, 0, 1:2].bitcast(F32), 0.0).then_inc(wf_ready, 1)
            n_loads = 4 + DEPTH * (2 + 4 + 1 + 2 * SB + 3 + 4 + 2)
            dve.wait_ge(in_loaded, 16 * n_loads)
            dve.tensor_copy(identb[:], ident)
            dve.tensor_copy(maskd[:], cmask[:, 0:P])
            dve.tensor_copy(masks[:], cmask[:, P:2 * P]).then_inc(consts_ready, 1)
            dve.wait_ge(freed[0], 3)
            lam = par_all[:, :, :].rearrange("p l (t r) -> p l t r", r=NR)[:, :, :, R_LAM]
            dve.scalar_tensor_tensor(out=spt[0][:], in0=lam, scalar=-1.0, in1=lam, op0=ALU.mult, op1=ALU.max).then_inc(pre_done, 1)
            dve.wait_ge(consts_ready, 2)
            log1p(spt[1][:], spt[2][:], spt[3][:], spt[4][:], spt[2][:])
            dve.tensor_scalar(spt[3][:], lam, -1.0, 0.0, ALU.mult, ALU.max)
            dve.drain()
            dve.tensor_tensor(spt[4][:], spt[3][:], spt[2][:], ALU.add)
            dve.drain()
            dve.tensor_scalar(decay[:, :, 0, :], spt[4][:], -8.0, None, ALU.mult)
            dve.tensor_scalar(decay[:, :, 1, :], spt[4][:], 8.0, None, ALU.mult)
            dve.wait_ge(freed[1], 3)
            for j in range(2):
                dve.wait_ge(hi_ready, j + 1)
                dve.tensor_tensor(split_tile(wlo, j), raw_tile(0, j), split_tile(whi, j).bitcast(F32), ALU.subtract).then_inc(lo_ready, 1)

            with dve.Fori(0, DEPTH) as L:
                dve.drain()
                dve.tensor_copy(gain[:], gains[:, bass.ds(L, 1), :].rearrange("p l n -> p (l n)"))
                dve.tensor_copy(bf[:], bfor[:, bass.ds(L, 1)])
                dve.tensor_copy(dk[:, :, :].rearrange("p a t -> p (a t)"), decay[:, bass.ds(L, 1), :, :].rearrange("p l a t -> p (l a t)"))
                dve.wait_ge(wf_hi, L + 1)
                dve.tensor_tensor(wfl[:, 0:KD * F_W], wfr[:, :, :].rearrange("p k c -> p (k c)"), wfh[:, 0:KD * F_W].bitcast(F32),
                                  ALU.subtract).then_inc(wf_ready, 1)
                dve.drain()
                dve.tensor_scalar(gain[:, 24:25], gain[:, 24:25], HD ** -0.5, None, ALU.mult)
                ffn("ffn1", 0, L)
                norm(S["mixnorm"], 1, L)

                fv = S["fv"]
                dve.memset(cp[:], 0.0)
                dve.memset(rhss[0:NS, PAST:PAST + NS], 0.0)
                dve.memset(rhss[NS:P, :], 1.0)
                for q in qeo:
                    dve.memset(q[:], 0.0)
                dve.wait_ge(lfp_loaded, L * (SB * NPG * 16) + SB * NPG * 16)
                dve.tensor_copy(lfp[:, :, NS:2 * NS], lfp[:, :, 0:NS]).then_inc(lfp_ready, 1)
                z, az, ez = tmp[0][0:F_W, 0:N], tmp[2][0:F_W, 0:N], tmp[3][0:F_W, 0:N]
                wait_tile(fv, 0, L)
                dve.tensor_scalar(two(z), ps[fv.slot(0)][0:F_W, :, 0:HF], bf[:, 0:1], None, ALU.add).then_inc(freed[fv.slot(0)], 1)
                dve.drain()
                dve.scalar_tensor_tensor(out=az, in0=z, scalar=-1.0, in1=z, op0=ALU.mult, op1=ALU.max).then_inc(absz_ready, 1)
                dve.wait_ge(expz_ready, L + 1)
                t1, t2, t3 = tmp[1][0:F_W, 0:N], tmp[4][0:F_W, 0:N], tmp[5][0:F_W, 0:N]
                log1p(ez, t1, t2, t3, az)
                dve.scalar_tensor_tensor(out=lf[:], in0=z, scalar=0.0, in1=az, op0=ALU.min, op1=ALU.subtract).then_inc(logf_ready, 1)
                split_ahead(fv, 0, L)
                split_ahead(fv, 1, L)
                dve.drain()
                c0, c1 = tmp[0][0:F_W, 0:SEQ], tmp[1][0:F_W, 0:SEQ]
                mid = tmp[2][0:F_W, 0:SEQ // 2].bitcast(BF16)
                dve.memset(tmp[6][:, 0:SEQ], 1.0)
                dve.drain()
                dve.tensor_tensor_scan(c0, tmp[6][0:F_W, 0:SEQ], lf[:, 0:SEQ], 0.0, ALU.mult, ALU.add)
                dve.drain()
                dve.tensor_copy(cp[0:F_W, :], c0)
                dve.drain()
                dve.tensor_tensor(c1, c0, cp[0:F_W, :], ALU.subtract)
                dve.drain()
                dve.tensor_copy(mid, c1)
                dve.drain()
                dve.tensor_copy(cp[32:32 + F_W, :], mid)
                dve.tensor_tensor(cp[64:64 + F_W, :], c1, mid, ALU.subtract)
                dve.drain()
                dve.tensor_scalar(ck[:], cp[:], const[0:96, C_M12:C_M12 + 1], const[0:96, C_M12 + 1:C_M12 + 2], ALU.mult, ALU.add)
                wait_tile(fv, 4, L)
                dve.tensor_tensor(tmp[3][:, 0:NS], ps[fv.slot(4)][:, 0, 0:NS], const[:, C_MREP:C_MREP + NS], ALU.mult)\
                    .then_inc(freed[fv.slot(4)], 1)
                dve.drain()
                dve.tensor_reduce(cs[:, PAST:PAST + ST], tmp[3][:, 0:NS].rearrange("p (s t) -> p t s", t=ST), AX.X, ALU.add)
                dve.drain()
                dve.wait_ge(freed[fv.slot(1)], fv.turn(1, L) + 1)
                dve.tensor_tensor_scan(cs[:], tmp[6][:, 0:PAST + ST], cs[:], 0.0, ALU.mult, ALU.add)
                dve.drain()
                dve.tensor_scalar(rhss[0:NS, 0:PAST], cs[0:NS, 0:PAST], -1.0, None, ALU.mult)
                for s in range(SB):
                    at = PAST + NS + s * ST
                    dve.tensor_scalar(rhss[0:NS, at:at + ST], cs[0:NS, PAST:PAST + ST], -1.0, None, ALU.mult)
                split_ahead(fv, 2, L)
                split_ahead(fv, 3, L)

                pr = S["pair"]
                with dve.Fori(0, PAIRS) as p:
                    it = L * PAIRS + p

                    def free(k):
                        return freed[pr.slot(k)]

                    split_ahead(pr, 0, L, p)
                    split_ahead(pr, 1, L, p)
                    dve.tensor_copy(prow[:], par_all[:, bass.ds(L, 1), bass.ds(p * NR, NR)].rearrange("p l n -> p (l n)"))
                    dve.tensor_copy(nbias[:], dk[:, :, bass.ds(p, 1)].rearrange("p a t -> p (a t)"))
                    for e in range(2):
                        at = (p * 2 + e) * 2 + C_SEL
                        dve.tensor_scalar(cq[e][:], cp[:], const[0:96, bass.ds(at, 1)], const[0:96, bass.ds(at + 1, 1)], ALU.mult, ALU.add)
                    dve.tensor_copy(lhss[0:NS, :], const[0:NS, bass.ds(p * P + C_IND, P)])
                    dve.tensor_tensor(lhss[NS:P, :].rearrange("p (a q) -> p a q", q=ST),
                                      const[NS:P, bass.ds(p * P + C_IND, P)].rearrange("p (a q) -> p a q", q=ST),
                                      cs[NS:P, PAST:PAST + ST].rearrange("p (a q) -> p a q", a=1).to_broadcast([NS, 16, ST]), ALU.mult)
                    for k, dst in ((4, qp), (5, kp)):
                        dve.wait_ge(free(k - 4), pr.turn(k - 4, L, p) + 1)
                        dve.wait_ge(free(k), pr.turn(k, L, p) + 1)
                        t = tmp[k - 4][:, 0:N]
                        dve.reciprocal(t, t)
                        dve.drain()
                        dve.scalar_tensor_tensor(out=dst[:], in0=dst[:], scalar=gain[:, 20 + k:21 + k], in1=t, op0=ALU.mult, op1=ALU.mult)
                    dve.drain()
                    for par in range(2):
                        for e in range(2):
                            hs = slice(HD * e, HD * (e + 1))
                            dst = qeo[par][hs, :].rearrange("p (a b h q) -> p a b h q", b=2, h=2, q=ST)[:, :, par, e, :]
                            src = qp[hs, SEQ:N].rearrange("p (a b q) -> p a b q", b=2, q=ST)[:, :, par, :]
                            ins = dve.tensor_copy(dst, src)
                    ins.then_inc(qk_ready, 1)

                    def taps(out, u, n, w0, kw, bias):
                        if bias is None:
                            dve.tensor_scalar(out[:, 0:n], u[:, 0:n], prow[:, w0:w0 + 1], None, ALU.mult)
                        else:
                            dve.tensor_scalar(out[:, 0:n], u[:, 0:n], prow[:, w0:w0 + 1], prow[:, bias:bias + 1], ALU.mult, ALU.add)
                        for j in range(1, kw):
                            dve.drain()
                            ins = dve.scalar_tensor_tensor(out=out[:, 0:n], in0=u[:, j:j + n], scalar=prow[:, w0 + j:w0 + j + 1],
                                                           in1=out[:, 0:n], op0=ALU.mult, op1=ALU.add)
                        return ins

                    split_ahead(pr, 2, L, p)
                    dve.wait_ge(free(6), pr.turn(6, L, p) + 1)
                    u = tmp[2]
                    dve.memset(u[:, 0:HB_], 0.0)
                    dve.tensor_copy(sequences(u, SB0, STEP_B, 0, HB_), prow[:, R_CS:R_CS + SB * HB_].rearrange("p (s r) -> p s r", r=HB_))
                    dve.drain()
                    taps(tmp[3], u, XB, R_CW, CONV_B, R_CB).then_inc(xc_ready, 1)
                    dve.tensor_copy(fcol[:, O_CP:O_CP + HB_], u[:, SEQ:SEQ + HB_])
                    dve.tensor_copy(fcol[:, O_CS:O_CS + SB * HB_].rearrange("p (s r) -> p s r", r=HB_), sequences(u, SB0, STEP_B, ST, HB_))
                    split_ahead(pr, 3, L, p)

                    for e in range(2):
                        for qb in range(QB):
                            k = 8 + 2 * e + qb // 2
                            if qb % 2 == 0:
                                wait_tile(pr, k, L, p)
                            dve.tensor_reduce(small[:, 32 + 4 * e + qb:33 + 4 * e + qb], ps[pr.slot(k)][:, qb % 2, 0:(qb + 1) * P], AX.X, ALU.max)
                        dve.drain()
                        dve.tensor_scalar(small[:, 4 * e:4 * e + 4], small[:, 32 + 4 * e:36 + 4 * e], -1.0, None, ALU.mult).then_inc(max_ready, 1)
                    wait_tile(pr, 12, L, p)
                    dve.tensor_reduce(small[:, 9:10], ps[pr.slot(12)][:, 0, 0:3 * P], AX.X, ALU.max)
                    dve.drain()
                    dve.tensor_scalar(small[:, 8:9], small[:, 9:10], -1.0, None, ALU.mult).then_inc(max_ready, 1)
                    for e in range(2):
                        dve.wait_ge(free(9 + 2 * e), pr.turn(9 + 2 * e, L, p) + 1)
                        dve.reciprocal(small[:, 40 + 4 * e:44 + 4 * e], small[:, 16 + 4 * e:20 + 4 * e])
                        dve.drain()
                        for qb in range(QB):
                            off, n = (0, P, 3 * P, 6 * P)[qb], (qb + 1) * P
                            ins = dve.tensor_scalar(prob[e][:, off:off + n], prob[e][:, off:off + n], small[:, 40 + 4 * e + qb:41 + 4 * e + qb], None, ALU.mult)
                        ins.then_inc(prob_ready, 1)
                    dve.wait_ge(exp_ready, it + 1)
                    dve.reciprocal(small[:, 10:11], small[:, 24:25])
                    dve.drain()
                    dve.tensor_scalar(probs[:], probs[:], small[:, 10:11], None, ALU.mult).then_inc(prob_ready, 1)

                    split_ahead(pr, 4, L, p)
                    wait_tile(pr, 14, L, p)
                    dve.wait_ge(free(13), pr.turn(13, L, p) + 1)
                    sx = ps[pr.slot(14)]
                    sc_ = tmp[5]
                    dve.memset(u[:, 0:HC_], 0.0)
                    cseq = u[:, SC0:SC0 + SB * STEP_C].rearrange("p (s c) -> p s c", c=STEP_C)
                    dve.tensor_tensor(u[:, HC_:HC_ + HF], sc_[:, 0:HF], sx[:, 0, 0:HF], ALU.mult)
                    dve.tensor_tensor(u[:, HC_ + HF:HC_ + SEQ], sc_[:, HF:SEQ], sx[:, 1, 0:SEQ - HF], ALU.mult)
                    dve.tensor_copy(cseq[:, :, 0:HC_], prow[:, R_SS:R_SS + SB * HC_].rearrange("p (s r) -> p s r", r=HC_))
                    dve.tensor_tensor(cseq[:, :, HC_:STEP_C], sc_[:, SEQ:N].rearrange("p (s t) -> p s t", t=ST),
                                      sx[:, 1, SEQ - HF:HF].rearrange("p (s t) -> p s t", t=ST), ALU.mult).then_inc(free(14), 1)
                    dve.drain()
                    uc = tmp[6]
                    taps(uc, u, XCW, R_SW, CONV_C, None)
                    dve.tensor_copy(fcol[:, O_SP:O_SP + HC_], u[:, SEQ:SEQ + HC_])
                    dve.tensor_copy(fcol[:, O_SS:O_SS + SB * HC_].rearrange("p (s r) -> p s r", r=HC_), cseq[:, :, ST:STEP_C])
                    split_ahead(pr, 5, L, p)

                    A, I_, R_, T_, XC_ = tmp[0], tmp[1], tmp[4], tmp[5], tmp[3]
                    dve.wait_ge(gates_ready, it + 1)
                    dve.scalar_tensor_tensor(out=T_[:, 0:XB], in0=R_[:, 0:XB], scalar=1.0, in1=T_[:, 0:XB], op0=ALU.add, op1=ALU.mult)\
                        .then_inc(root_in, 1)
                    dve.tensor_tensor(I_[:, 0:XB], I_[:, 0:XB], XC_[:, 0:XB], ALU.mult)
                    dve.drain()
                    dve.wait_ge(root_ready, it + 1)
                    dve.tensor_tensor(I_[:, 0:XB], I_[:, 0:XB], T_[:, 0:XB], ALU.mult)

                    dve.tensor_tensor(small[:, 48:56], one_each(A, 0), prow[:, R_H0:R_H0 + SB], ALU.mult)
                    dve.drain()
                    dve.tensor_tensor(one_each(I_, 0), one_each(I_, 0), small[:, 48:56], ALU.add)
                    dve.memset(one_each(A, 0), 0.0)
                    dve.drain()
                    dve.tensor_tensor_scan(R_[:, 0:XB], A[:, 0:XB], I_[:, 0:XB], 0.0, ALU.mult, ALU.add)
                    dve.drain()
                    dve.wait_ge(free(7), pr.turn(7, L, p) + 1)
                    og = o[:, bass.ds(p + 4, 1), :].rearrange("p a n -> p (a n)")
                    dve.tensor_tensor(og[:, 0:SEQ], R_[:, 0:SEQ], og[:, 0:SEQ], ALU.mult)
                    ogs = o[:, bass.ds(p + 4, 1), SEQ:N].rearrange("p a (s t) -> p (a s) t", t=ST)
                    dve.tensor_tensor(ogs, sequences(R_, SB0, STEP_B, 0, ST), ogs, ALU.mult)
                    dve.tensor_copy(fcol[:, O_HP:O_HP + 1], R_[:, SEQ - 1:SEQ])
                    dve.tensor_copy(fcol[:, O_HS:O_HS + SB], one_each(R_, ST - 1))
                    split_ahead(pr, 6, L, p)
                    split_ahead(pr, 7, L, p)
                    wait_tile(pr, 19, L, p)
                    sbp = ps[pr.slot(19)]
                    oc = o[:, bass.ds(p + 8, 1), :].rearrange("p a n -> p (a n)")
                    dve.tensor_tensor(oc[:, 0:HF], uc[:, 0:HF], sbp[:, 0, 0:HF], ALU.mult)
                    dve.tensor_tensor(oc[:, HF:SEQ], uc[:, HF:SEQ], sbp[:, 1, 0:SEQ - HF], ALU.mult)
                    ocs = o[:, bass.ds(p + 8, 1), SEQ:N].rearrange("p a (s t) -> p (a s) t", t=ST)
                    dve.tensor_tensor(ocs, sequences(uc, SC0, STEP_C, 0, ST), sbp[:, 1, SEQ - HF:HF].rearrange("p (s t) -> p s t", t=ST), ALU.mult).then_inc(free(19), 1)
                    dve.drain()
                    dve.tensor_copy(fout[:, bass.ds(p, 1), :].rearrange("p a n -> p (a n)"), fcol[:])
                    dve.drain()
                dve.drain().then_inc(f_ready, 1)

                for c in range(12):
                    dve.wait_ge(oh_ready, L * 12 + (c + 1))
                    dve.tensor_tensor(ol[:, c, :], o[:, c, :], oh[:, c, :].bitcast(F32), ALU.subtract).then_inc(o_ready, 1)
                mg = S["merge"]
                with dve.Fori(0, mg.steps) as i:
                    for b in range(3):
                        for j in range(4):
                            k = 4 * b + j
                            split_ahead(mg, k, L, i)
                            if j < 2:
                                continue
                            wait_tile(mg, k, L, i)
                            dve.wait_ge(freed[mg.slot(k - 2)], mg.turn(k - 2, L, i) + 1)
                            mt = merged[:, bass.ds(i * 2 + (j - 2), 1), :].rearrange("p a (b n) -> p (a b) n", b=2)
                            if b == 0:
                                dve.tensor_tensor(mt, two(tmp[j - 2][:, 0:N]), cols(mg.slot(k)), ALU.mult).then_inc(freed[mg.slot(k)], 1)
                            else:
                                t = two(tmp[2 + j][:, 0:N])
                                dve.tensor_tensor(t, two(tmp[j - 2][:, 0:N]), cols(mg.slot(k)), ALU.mult).then_inc(freed[mg.slot(k)], 1)
                                dve.drain()
                                dve.tensor_tensor(mt, mt, t, ALU.add)
                dve.drain().then_inc(merged_ready, 1)
                for c in range(KD):
                    dve.wait_ge(mh_ready, L * 8 + (c + 1))
                    dve.tensor_tensor(hl[:, c, :], merged[:, c, :], hh[:, c, :].bitcast(F32), ALU.subtract).then_inc(m_ready, 1)
                update(S["out"], L, 1.0)
                ffn("ffn2", 2, L)
                dve.wait_ge(f_stored, L * 96 + 96)

        @block.gpsimd
        def _(pool):
            def add_squares(base):
                for m in range(KD):
                    if m == 0:
                        wait_apart(pool, sq_ready, base + (m + 1))
                        pool.tensor_copy(tmp[6][:, 0:N], tmp[2][:, 0:N]).then_inc(sq_added, 1)
                    else:
                        pool.drain()
                        pool.wait_ge(sq_ready, base + (m + 1))
                        pool.tensor_tensor(tmp[6][:, 0:N], tmp[6][:, 0:N], tmp[2 + m % 2][:, 0:N], ALU.add).then_inc(sq_added, 1)

            add_squares(0)
            with pool.Fori(0, DEPTH) as L:
                add_squares(L * 24 + 8)
                fv, pr, st = S["fv"], S["pair"], S["state"]
                for k in (2, 3, 5, 6):
                    wait_apart(pool, freed[fv.slot(k)], fv.turn(k, L) + 1)
                dst = t_out["prompt_v"].rearrange("a l (b p) h d -> l p (a b) (h d)", p=P)[bass.ds(L, 1)]
                pool.dma_start(dst.rearrange("l p b n -> p (l b) n"), vtok[:, 0:4, :]).then_inc(v_stored, 16)
                dst = t_out["sample_v"].rearrange("s l t h d -> l s t (h d)")[bass.ds(L, 1)].rearrange("l s t n -> (l s) t n")
                pool.dma_start(dst, vtok[NS:P, 4, :]).then_inc(v_stored, 16)
                wait_apart(pool, freed[fv.slot(7)], fv.turn(7, L) + 1)
                dst = t_out["prompt_logf"].rearrange("a l (b p) h -> l p (a b) h", p=P)[bass.ds(L, 1)]
                pool.dma_start(dst.rearrange("l p b n -> p (l b) n"), lfo[:, 0:4, :]).then_inc(lf_stored, 16)
                dst = t_out["sample_logf"].rearrange("s l t h -> l s t h")[bass.ds(L, 1)].rearrange("l s t n -> (l s) t n")
                pool.dma_start(dst, lfo[NS:P, 4, :]).then_inc(lf_stored, 16)
                with pool.Fori(0, PAIRS) as p:
                    wait_apart(pool, filled[pr.slot(12)], pr.turn(12, L, p) + 1)
                    pool.tensor_copy(vp[:], vtok[:, :, bass.ds(p * P, P)]).then_inc(vp_ready, 1)
                    wait_apart(pool, freed[pr.slot(12)], pr.turn(12, L, p) + 1)
                    dst = t_out["prompt_k"].rearrange("a l (b p) h d -> l p (a b) (h d)", p=P)[bass.ds(L, 1), :, :, bass.ds(p * P, P)]
                    pool.dma_start(dst.rearrange("l p b n -> p (l b) n"), kout[:, 0:4, :]).then_inc(k_stored, 16)
                    dst = t_out["sample_k"].rearrange("s l t h d -> l s t (h d)")[bass.ds(L, 1), :, :, bass.ds(p * P, P)]
                    pool.dma_start(dst.rearrange("l s t n -> (l s) t n"), kout[NS:P, 4, :])\
                        .then_inc(k_stored, 16)
                wait_apart(pool, freed[st.slot(0)], st.turn(0, L) + 1)
                for name, r, n in (("prompt_lru_h", O_HP, 1), ("prompt_lru_conv", O_CP, HB_), ("prompt_sc_conv", O_SP, HC_),
                                   ("sample_lru_h", O_HS, SB), ("sample_lru_conv", O_CS, HB_), ("sample_sc_conv", O_SS, HC_)):
                    out = t_out[name]
                    if len(out.shape) == 3:
                        dst = out[:, bass.ds(L, 1), :].rearrange("s l n -> (s l) n")
                        pool.dma_start(dst, frow[r:r + n, :]).then_inc(f_stored, 16)
                    elif name.startswith("prompt"):
                        dst = out[:, bass.ds(L, 1), :, :].rearrange("s l r n -> (s l r) n")
                        pool.dma_start(dst, frow[r:r + n, :]).then_inc(f_stored, 16)
                    else:
                        dst = out[:, bass.ds(L, 1), :, :].rearrange("s l r n -> (s l) r n")
                        pool.dma_start(dst, frow[r:r + n * SB, :]).then_inc(f_stored, 16)
                add_squares(L * 24 + 16)
                add_squares(L * 24 + 24)




def constants():
    c = np.zeros((P, NCONST), np.float32)
    r = np.arange(P)
    c[:, C_ID:C_ID + P] = np.eye(P)
    c[:, C_ONE:C_ONE + P] = 1.0 / D
    c[:, C_BONE:C_BONE + P] = (r[:, None] // HD == r[None] // HD) / HD
    row_s, row_h = r % NS // H, r % H
    col_s, col_h, col_q = r // 16, r // ST % 2, r % ST
    for p in range(PAIRS):
        c[:, C_IND + p * P:C_IND + (p + 1) * P] = (row_s[:, None] == col_s) & (row_h[:, None] == 2 * p + col_h)
    n = np.arange(NS)
    c[:, C_MREP:C_MREP + NS] = row_s[:, None] == n // ST
    c[:H, C_REP:C_REP + P] = np.arange(H)[:, None] == r % H
    part = r % 32
    for h in range(H):
        c[:96, C_SEL + 2 * h] = (part == H + h)[:96]
        c[:96, C_SEL + 2 * h + 1] = (part == h)[:96]
    c[:96, C_M12] = -(part < H)[:96].astype(np.float32)
    c[:96, C_M12 + 1] = ((part >= H) & (part < 2 * H))[:96]
    c[:, C_MD:C_MD + P] = np.where(r[None] <= r[:, None], 0.0, NEG)
    key_s, key_t = (r - NS) // ST, (r - NS) % ST
    seen = (r[None] >= NS) & (key_s[None] == col_s[:, None]) & (key_t[None] <= col_q[:, None])
    c[:, C_MS:C_MS + P] = np.where(seen, 0.0, NEG)
    return c


_OUTS = [
    ("y_prompt", (1, SEQ, D)), ("y_sample", (SB, ST, D)),
    ("prompt_k", (1, DEPTH, SEQ, H, HD)), ("prompt_v", (1, DEPTH, SEQ, H, HD)), ("prompt_logf", (1, DEPTH, SEQ, H)),
    ("prompt_lru_h", (1, DEPTH, WID)), ("prompt_lru_conv", (1, DEPTH, HB_, WID)), ("prompt_sc_conv", (1, DEPTH, HC_, WID)),
    ("sample_k", (SB, DEPTH, ST, H, HD)), ("sample_v", (SB, DEPTH, ST, H, HD)), ("sample_logf", (SB, DEPTH, ST, H)),
    ("sample_lru_h", (SB, DEPTH, WID)), ("sample_lru_conv", (SB, DEPTH, HB_, WID)), ("sample_sc_conv", (SB, DEPTH, HC_, WID)),
]


def kernel(**inputs):
    import numpy as _np
    import concourse.bacc as _bacc
    from concourse import mybir as _mybir
    from concourse.bass_utils import run_bass_kernel_spmd as _run

    nc = _bacc.Bacc("TRN2", target_bir_lowering=False, num_devices=1)
    arrays = {f"in_{name}": _np.ascontiguousarray(a) for name, a in inputs.items()}
    arrays["in_const_table"] = constants()
    t_in = {name[3:]: nc.dram_tensor(name, a.shape, _mybir.dt.from_np(a.dtype), kind="ExternalInput").ap()
            for name, a in arrays.items()}
    t_out = {name: nc.dram_tensor(f"out_{name}", shape, _mybir.dt.float32, kind="ExternalOutput").ap()
             for name, shape in _OUTS}
    build(nc, t_in, t_out)
    r = _run(nc, [arrays], core_ids=[0])
    return tuple(r.results[0][f"out_{name}"] for name, _ in _OUTS)
```

```python
from contextlib import ExitStack

import concourse.bass as bass
import numpy as np
from concourse import mybir

F32 = mybir.dt.float32
F32R = mybir.dt.float32r
BF16 = mybir.dt.bfloat16
I32 = mybir.dt.int32
ALU = mybir.AluOpType
ACT = mybir.ActivationFunctionType
AX = mybir.AxisListType

P = 128
D = 1024
KD = D // P
DEPTH = 2
SEQ = 512
QB = SEQ // P
SB, ST = 8, 8
NS = SB * ST
N = SEQ + NS
HF = N // 2
H, HD = 8, 64
PAIRS = H // 2
WID = 512
FFN = 2816
EPS = 1e-6
PAGE = 128
NPG = 2
PAST = NPG * PAGE
N_IN = 3 * WID + H + 2 * WID + 3 * WID + 3 * D
COL_Q, COL_K, COL_V, COL_F = 0, WID, 2 * WID, 3 * WID
COL_BX = COL_F + H
COL_BY, COL_SB, COL_SC, COL_SX, COL_G = (COL_BX + WID * n for n in range(1, 6))
CONV_B, CONV_C = 4, 3
HB_, HC_ = CONV_B - 1, CONV_C - 1
STEP_B, STEP_C = HB_ + ST, HC_ + ST
UB, UC = HB_ + SEQ + SB * STEP_B, HC_ + SEQ + SB * STEP_C
XB, XCW = UB - HB_, UC - HC_
SB0, SC0 = HB_ + SEQ, HC_ + SEQ
R_CW, R_CB, R_BA, R_BX, R_LAM, R_SW, R_H0, R_CS, R_SS, NR = 0, 4, 5, 6, 7, 8, 11, 19, 43, 59
O_HP, O_CP, O_SP, O_HS, O_CS, O_SS, NO = 0, 1, 4, 6, 14, 38, 54
C_ID, C_ONE, C_BONE, C_IND, C_MREP, C_REP, C_SEL, C_M12 = 0, 128, 256, 384, 896, 960, 1088, 1104
C_KEEP = 1106
C_MD, C_MS = C_KEEP, C_KEEP + P
NCONST = C_KEEP + 2 * P
NEG = -1e30
F_W = 2 * H


X_LOADS, IN_LOADS = 3, 21


class Stage:

    def __init__(self, plan, steps, units, tiles):
        assert steps == 1 or (units % 2 == 0 and tiles % 4 == 0)
        self.steps, self.units, self.tiles = steps, units, tiles
        self.first_unit, self.first_tile = plan["units"], plan["tiles"]
        plan["units"] += steps * units
        plan["tiles"] += steps * tiles
        self.plan = plan

    def slot(self, k):
        return (self.first_tile + k) % 4

    def turn(self, k, layer, step=0):
        whole = self.plan["layer_tiles"] // 4
        return layer * whole + step * (self.tiles // 4) + (self.plan["before"] + self.first_tile + k) // 4

    def unit(self, k, layer, step=0):
        return layer * self.plan["layer_units"] + step * self.units + self.first_unit + k

    def unit_slot(self, k):
        return (self.first_unit + k) % 2


AHEAD = 3
PRE_TILES = 12


def make_plan():
    plan = {"units": 0, "tiles": 0, "before": PRE_TILES, "layer_tiles": 0, "layer_units": 0}
    s = {}

    def ffn(name):
        s[name + "norm"] = Stage(plan, 1, 0, 1)
        s[name] = []
        for pairs in (4, 4, 3):
            s[name].append((Stage(plan, pairs, 2, 4), Stage(plan, 2, 2, 4), 2 * pairs))

    ffn("ffn1")
    s["mixnorm"] = Stage(plan, 1, 0, 1)
    s["fv"] = Stage(plan, 1, 2, 8)
    s["pair"] = Stage(plan, PAIRS, 4, 24)
    s["state"] = Stage(plan, 1, 0, 1)
    s["merge"] = Stage(plan, 4, 6, 12)
    s["out"] = Stage(plan, 2, 2, 4)
    ffn("ffn2")
    plan["tiles_used"] = plan["tiles"]
    plan["tiles"] += -plan["tiles"] % 4
    plan["layer_tiles"], plan["layer_units"] = plan["tiles"], plan["units"]
    assert plan["units"] % 2 == 0
    return s, plan


def sequences(buf, first, step, at, n):
    return buf[:, first:first + SB * step].rearrange("p (s c) -> p s c", c=step)[:, :, at:at + n]


def one_each(buf, at):
    return buf[:, SB0:SB0 + SB * STEP_B].rearrange("p (s c) -> p s c", c=STEP_B)[:, :, at]


def build(nc, t_in, t_out):
    S, plan = make_plan()
    with ExitStack() as ctx:
        ctx.enter_context(nc.allow_non_contiguous_dma(reason="one value per partition: forget biases"))

        def sem(name):
            return ctx.enter_context(nc.semaphore(name))

        def sb(name, shape, dt=F32, where=ctx):
            return where.enter_context(nc.sbuf_tensor(name, shape, dt))

        ps = [ctx.enter_context(nc.psum_tensor(f"ps{i}", [P, 2, 512], F32)) for i in range(4)]

        x = sb("x", [P, KD, N])
        hh = sb("hh", [P, KD, N], F32R)
        hl = sb("hl", [P, KD, N], F32R)
        wraw = sb("wraw", [P, 2, KD * 256])
        whi = sb("whi", [P, 2, KD * P], F32R)
        wlo = sb("wlo", [P, 2, KD * P], F32R)
        const = sb("const", [P, C_KEEP])
        identb = sb("identb", [P, P], BF16)
        maskd = sb("maskd", [P, P], BF16)
        masks = sb("masks", [P, P], BF16)
        par_all = sb("par_all", [P, DEPTH, 4 * NR])
        gains = sb("gains", [P, DEPTH + 1, 26])
        gain = sb("gain", [P, 26])
        bfor = sb("bfor", [F_W, DEPTH])
        bf = sb("bf", [F_W, 1])
        decay = sb("decay", [P, DEPTH, 2, 4])
        dk = sb("dk", [P, 2, 4])
        nbias = sb("nbias", [P, 2])
        eps = sb("eps", [P, 2])
        pages = sb("pages", [1, SB * NPG], I32)
        wfr = sb("wfr", [P, KD, F_W])
        wfh = sb("wfh", [P, KD * F_W + P - F_W], F32R)
        wfl = sb("wfl", [P, KD * F_W + P - F_W], F32R)
        wab = sb("wab", [P, 2, P])
        small = sb("small", [P, 64])
        tmp = [sb(f"tmp{i}", [P, UB + 1]) for i in range(7)]
        ident = const[:, C_ID:C_ID + P]
        ones = const[:, C_ONE:C_ONE + P]
        bones = const[:, C_BONE:C_BONE + P]

        with ExitStack() as m:
            ah = sb("ah", [P, 8, N], F32R, m)
            al = sb("al", [P, 8, N], F32R, m)
        with ExitStack() as m:
            xin = sb("xin", [P, 5, D], F32, m)
            rows = sb("rows", [NR, DEPTH, WID], F32, m)
            rowsg = sb("rowsg", [26, DEPTH, P], F32, m)
            cmask = sb("cmask", [P, 2 * P], F32, m)
            spt = [sb(f"spt{i}", [P, DEPTH, 4], F32, m) for i in range(5)]
        with ExitStack() as m:
            yout = sb("yout", [P, 5, D], F32, m)
        with ExitStack() as m:
            o = sb("o", [P, 12, N], F32, m)
            with ExitStack() as m2:
                kv = sb("kv", [P, SB * NPG, P], F32, m2)
                kpt = sb("kpt", [P, SB * PAST], F32, m2)
                prob = [sb(f"prob{i}", [P, 10 * P], F32, m2) for i in range(2)]
                probt = sb("probt", [P, 10 * P], F32, m2)
                probs = sb("probs", [P, 3 * P], F32, m2)
                probst = sb("probst", [P, 3 * P], F32, m2)
                qp = sb("qp", [P, N], F32, m2)
                kp = sb("kp", [P, N], F32, m2)
                cp = sb("cp", [96, SEQ], BF16, m2)
                ck = sb("ck", [96, SEQ], BF16, m2)
                cq = [sb(f"cq{i}", [96, SEQ], BF16, m2) for i in range(2)]
                rhss = sb("rhss", [P, 3 * P], F32, m2)
                lhss = sb("lhss", [P, P], F32, m2)
                qeo = [sb(f"qeo{i}", [P, P], F32, m2) for i in range(2)]
                cs = sb("cs", [P, PAST + ST], F32, m2)
                lfp = sb("lfp", [P, NPG, 2 * NS], F32, m2)
                lf = sb("lf", [F_W, N], F32, m2)
                vp = sb("vp", [P, 5, P], F32, m2)
                vtok = sb("vtok", [P, 5, WID], F32, m2)
                kout = sb("kout", [P, 5, P], F32, m2)
                lfo = sb("lfo", [P, 5, H], F32, m2)
                fcol = sb("fcol", [P, NO], F32, m2)
                fout = sb("fout", [P, 4, NO], F32, m2)
                prow = sb("prow", [P, NR], F32, m2)
            with ExitStack() as m2:
                oh = sb("oh", [P, 12, N], F32R, m2)
                merged = sb("merged", [P, KD, N], F32, m2)
                frow = sb("frow", [NO, WID], F32, m2)
                mh = sb("mh", [P, KD, N], F32R, m2)
        with ExitStack() as m:
            ol = sb("ol", [P, 12, N], F32R, m)
            sb("over_oh", [P, 12, N], F32R, m)
            ml = sb("ml", [P, KD, N], F32R, m)

        x_loaded = sem("x_loaded")
        in_loaded, pages_loaded = sem("in_loaded"), sem("pages_loaded")
        unit_loaded = [sem(f"unit_loaded{i}") for i in range(2)]
        hi_ready, lo_ready = sem("hi_ready"), sem("lo_ready")
        filled = [sem(f"filled{i}") for i in range(4)]
        freed = [sem(f"freed{i}") for i in range(4)]
        consts_ready = sem("consts_ready")
        pre_done = sem("pre_done")
        sq_ready, sq_added = sem("sq_ready"), sem("sq_added")
        rstd_ready, hh_ready, h_ready = sem("rstd_ready"), sem("hh_ready"), sem("h_ready")
        by_ready, gelu_ready, gate_ready = sem("by_ready"), sem("gelu_ready"), sem("gate_ready")
        silu_ready, a_ready = sem("silu_ready"), sem("a_ready")
        wf_loaded, wf_hi, wf_ready = sem("wf_loaded"), sem("wf_hi"), sem("wf_ready")
        lfp_loaded, lfp_ready = sem("lfp_loaded"), sem("lfp_ready")
        absz_ready, expz_ready, logf_ready = sem("absz_ready"), sem("expz_ready"), sem("logf_ready")
        v_stored, k_stored, lf_stored, f_stored = sem("v_stored"), sem("k_stored"), sem("lf_stored"), sem("f_stored")
        kv_loaded, wab_loaded = sem("kv_loaded"), sem("wab_loaded")
        qk_squared, qk_ready = sem("qk_squared"), sem("qk_ready")
        xc_ready = sem("xc_ready")
        max_ready, exp_ready, prob_ready = sem("max_ready"), sem("exp_ready"), sem("prob_ready")
        pv_done, vp_ready = sem("pv_done"), sem("vp_ready")
        gates_ready, root_in, root_ready = sem("gates_ready"), sem("root_in"), sem("root_ready")
        f_ready = sem("f_ready")
        oh_ready, o_ready = sem("oh_ready"), sem("o_ready")
        m_ready = sem("m_ready")
        y_stored = sem("y_stored")

        def wait_apart(eng, what, value):
            if not isinstance(value, int):
                value = eng.snap(value)
                eng.compute_val(value)
            eng.wait_ge(pre_done, 1)
            eng.wait_ge(what, value)

        def cols(k):
            return ps[k][:, :, 0:HF]

        def chunk(buf, at):
            return buf[:, bass.ds(at, 1), :].rearrange("p a n -> p (a n)")

        def norm_gain(L, at):
            return gains[:, bass.ds(L, 1), bass.ds(at, 1)].rearrange("p l n -> p (l n)")

        def two(ap):
            return ap.rearrange("p (b n) -> p b n", b=2)

        def raw_tile(u, j, rowwise=False):
            if rowwise:
                return wraw[:, u, j * 4 * P:(j + 1) * 4 * P].rearrange("p (k c) -> p k c", c=P)
            return wraw[:, u, :].rearrange("p (k c) -> p k c", c=256)[:, :, j * P:(j + 1) * P]

        def split_tile(buf, j, rowwise=False):
            n = 4 if rowwise else KD
            return buf[:, j, 0:n * P].rearrange("p (k c) -> p k c", c=P)

        def ahead(st, k):
            k2 = k + 2
            rowwise = st is S["pair"] and k2 in (6, 7)
            return k2 // 2, k2 % 2, rowwise

        block = ctx.enter_context(nc.Block())

        @block.sync
        def _(sp):
            sp.dma_start(const[:, :], t_in["const_table"][:, 0:C_KEEP]).then_inc(x_loaded, 16)
            sp.dma_start(xin[:, 0:4, :], t_in["x_prompt"].rearrange("a (b p) d -> p (a b) d", p=P)).then_inc(x_loaded, 16)
            sp.dma_start(xin[0:NS, 4, :], t_in["x_sample"].rearrange("s t d -> (s t) d")).then_inc(x_loaded, 16)
            for n, name in enumerate(("ffn1_norm", "mix_norm", "ffn2_norm")):
                sp.dma_start(rowsg[8 * n:8 * n + 8, :, :], t_in[name].rearrange("l (k p) -> k l p", p=P)).then_inc(in_loaded, 16)
            for n, name in enumerate(("q_norm", "k_norm")):
                for e in range(2):
                    sp.dma_start(rowsg[24 + n:25 + n, :, HD * e:HD * (e + 1)], t_in[name].rearrange("(a l) d -> a l d", a=1)).then_inc(in_loaded, 16)
            for name, r, n in (("lru_conv_w", R_CW, CONV_B), ("sc_conv_w", R_SW, CONV_C)):
                sp.dma_start(rows[r:r + n, :, :], t_in[name].rearrange("l r n -> r l n")).then_inc(in_loaded, 16)
            for name, r in (("lru_conv_b", R_CB), ("lru_ba", R_BA), ("lru_bx", R_BX), ("lru_lambda", R_LAM)):
                sp.dma_start(rows[r:r + 1, :, :], t_in[name].rearrange("(a l) n -> a l n", a=1)).then_inc(in_loaded, 16)
            sp.dma_start(rows[R_H0:R_H0 + SB, :, :], t_in["state_lru_h"]).then_inc(in_loaded, 16)
            for name, r, n in (("state_lru_conv", R_CS, HB_), ("state_sc_conv", R_SS, HC_)):
                for l in range(DEPTH):
                    sp.dma_start(rows[r:r + n * SB, l, :], t_in[name][:, l, :, :]).then_inc(in_loaded, 16)
            for e in range(2):
                sp.dma_start(bfor[H * e:H * (e + 1), :], t_in["b_forget"].rearrange("l h -> h l")).then_inc(in_loaded, 16)
            sp.dma_start(cmask[:, :], t_in["const_table"][:, C_KEEP:NCONST]).then_inc(in_loaded, 16)
            sp.dma_start(pages[:], t_in["page_table"].rearrange("s g -> (s g)").rearrange("(a n) -> a n", a=1)).then_inc(pages_loaded, 16)

            def load(st, k, L, i, *parts):
                n = st.unit(k, L, i)
                u = st.unit_slot(k)
                sp.wait_ge(lo_ready, n * 2 - 2 + AHEAD)
                at = 0
                for name, k0, kc, c0, nc_ in parts:
                    src = t_in[name].rearrange("l (k p) n -> l p k n", p=P)[bass.ds(L, 1), :, k0:k0 + kc, bass.ds(c0, nc_)]
                    width = sum(q[4] for q in parts)
                    dst = wraw[:, u, 0:KD * width].rearrange("p (k c) -> p k c", c=width)[:, 0:kc, at:at + nc_]
                    sp.dma_start(dst, src.rearrange("l p k n -> p (l k) n")).then_inc(unit_loaded[u], 32 // len(parts))
                    at += nc_

            def ffn(name, L):
                w1, w2 = name + "_w_in", name + "_w_out"
                done = 0
                for st_in, st_out, kc in S[name]:
                    with sp.Fori(0, st_in.steps) as i:
                        load(st_in, 0, L, i, (w1, 0, KD, i * 256 + done * P, 256))
                        load(st_in, 1, L, i, (w1, 0, KD, i * 256 + (done * P + FFN), 256))
                    with sp.Fori(0, 2) as i:
                        for k in range(2):
                            load(st_out, k, L, i, (w2, done, kc, i * 512 + 256 * k, 256))
                    if name == "ffn1" and done == 0:
                        past_forgets(L)
                    done += kc

            def past_forgets(L):
                norm = S["ffn1norm"]
                wait_apart(sp, filled[norm.slot(0)], norm.turn(0, L) + 1)
                sp.wait_ge(pages_loaded, 16)
                for s in range(SB):
                    for g in range(NPG):
                        page = sp.value_load(pages[0:1, s * NPG + g:s * NPG + g + 1], min_val=0, max_val=t_in["cache_k"].shape[0] - 1)
                        src = t_in["cache_logf"][bass.ds(page, 1), bass.ds(L, 1), :, :].rearrange("a b t h -> (a b t) h")
                        sp.dma_start(lfp[:, g, s * H:(s + 1) * H], src).then_inc(lfp_loaded, 16)

            with sp.Fori(0, DEPTH) as L:
                sp.wait_ge(wf_ready, L + 1)
                for e in range(2):
                    src = t_in["w_in"].rearrange("l (k p) n -> l p k n", p=P)[bass.ds(L, 1), :, :, COL_F:COL_F + H]
                    sp.dma_start(wfr[:, :, H * e:H * (e + 1)], src.rearrange("l p k n -> p (l k) n")).then_inc(wf_loaded, 16)
                ffn("ffn1", L)
                fv = S["fv"]
                for k in range(2):
                    load(fv, k, L, 0, ("w_in", 0, KD, COL_V + 256 * k, 256))
                pr = S["pair"]
                with sp.Fori(0, PAIRS) as p:
                    def pages_of(name):
                        for s in range(SB):
                            for g in range(NPG):
                                page = sp.value_load(pages[0:1, s * NPG + g:s * NPG + g + 1], min_val=0, max_val=t_in["cache_k"].shape[0] - 1)
                                src = t_in[name].rearrange("a l t h d -> a l t (h d)")[bass.ds(page, 1), bass.ds(L, 1), :, bass.ds(p * P, P)]
                                sp.dma_start(kv[:, s * NPG + g, :], src.rearrange("a b t n -> (a b t) n")).then_inc(kv_loaded, 16)

                    load(pr, 0, L, p, ("w_in", 0, KD, p * P + COL_Q, P), ("w_in", 0, KD, p * P + COL_K, P))
                    load(pr, 1, L, p, ("w_in", 0, KD, p * P + COL_BX, P), ("w_in", 0, KD, p * P + COL_BY, P))
                    load(pr, 2, L, p, ("w_in", 0, KD, p * P + COL_SC, P), ("w_in", 0, KD, p * P + COL_SX, P))
                    wait_apart(sp, filled[pr.slot(21)], pr.turn(21, L, p) - 5)
                    for j, name in enumerate(("lru_wa", "lru_wx")):
                        for e in range(2):
                            src = t_in[name][bass.ds(L, 1), bass.ds(p * 2 + e, 1), :, :].rearrange("a b i j -> (a b i) j")
                            sp.dma_start(wab[HD * e:HD * (e + 1), j, HD * e:HD * (e + 1)], src).then_inc(wab_loaded, 16)
                    pages_of("cache_k")
                    load(pr, 3, L, p, ("w_in", 0, KD, p * P + COL_SB, P))
                    wait_apart(sp, filled[pr.slot(8)], pr.turn(8, L, p) + 1)
                    pages_of("cache_v")
                mg = S["merge"]
                with sp.Fori(0, mg.steps) as i:
                    for b in range(3):
                        load(mg, 2 * b, L, i, ("w_in", 0, KD, i * 256 + (COL_G + D * b), 256))
                        load(mg, 2 * b + 1, L, i, ("w_branch", 4 * b, 4, i * 256, 256))
                with sp.Fori(0, 2) as i:
                    for k in range(2):
                        load(S["out"], k, L, i, ("w_out", 0, KD, i * 512 + 256 * k, 256))
                ffn("ffn2", L)
            sp.wait_ge(lo_ready, 2 * DEPTH * plan["layer_units"] - 2 + AHEAD)
            src = t_in["w_out"].rearrange("l (k p) n -> l p k n", p=P)[0, :, :, 0:256]
            sp.dma_start(wraw[:, 0, :].rearrange("p (k c) -> p k c", c=256), src).then_inc(unit_loaded[0], 32)
            post = DEPTH * plan["layer_tiles"] + PRE_TILES
            for b in range(5):
                sp.wait_ge(freed[(post + b) % 4], (post + b) // 4 + 1)
                if b < 4:
                    sp.dma_start(t_out["y_prompt"][0, b * P:(b + 1) * P, :], yout[:, b, :]).then_inc(y_stored, 16)
                else:
                    sp.dma_start(t_out["y_sample"].rearrange("s t d -> (s t) d"), yout[NS:P, b, :]).then_inc(y_stored, 16)
            sp.wait_ge(y_stored, 5 * 16)
            sp.wait_ge(v_stored, DEPTH * 32)
            sp.wait_ge(k_stored, DEPTH * PAIRS * 32)
            sp.wait_ge(lf_stored, DEPTH * 32)
            sp.wait_ge(f_stored, DEPTH * 96)

        @block.tensor
        def _(pe):
            def wait_psum(st, k, L, i=0):
                pe.wait_ge(freed[st.slot(k)], st.turn(k, L, i))

            def wait_weights(st, w, L, i=0):
                pe.wait_ge(lo_ready, st.unit(0, L, i) * 2 + (w + 1 + AHEAD))

            def project(slot, w, chunks, rhs_hi, rhs_lo, start=True, stop=True, before=None):
                for c, k in enumerate(chunks):
                    if before is not None:
                        before(c)
                    wh, wl = whi[:, w % 2, c * P:(c + 1) * P], wlo[:, w % 2, c * P:(c + 1) * P]
                    for n, (weights, rhs) in enumerate(((wh, rhs_hi), (wh, rhs_lo), (wl, rhs_hi))):
                        for half in range(2):
                            last = pe.matmul(ps[slot][:, half, 0:HF], weights, rhs[:, k, half * HF:(half + 1) * HF],
                                             start=(start and c == 0 and n == 0), stop=(stop and c == len(chunks) - 1 and n == 2))
                return last

            def plain(st, k, w, chunks, rhs_hi, rhs_lo, L, i=0, before=None):
                wait_weights(st, w, L, i)
                wait_psum(st, k, L, i)
                project(st.slot(k), w, chunks, rhs_hi, rhs_lo, before=before).then_inc(filled[st.slot(k)], 1)

            def norm(st, n, L):
                pe.wait_ge(sq_added, L * 24 + 8 * (n + 1))
                wait_psum(st, 0, L)
                for half in range(2):
                    last = pe.matmul(ps[st.slot(0)][:, half, 0:HF], ones, tmp[6][:, half * HF:half * HF + HF],
                                     start=True, stop=True)
                last.then_inc(filled[st.slot(0)], 1)

            def ffn(name, n, L):
                def chunk_ready(c):
                    pe.wait_ge(h_ready, L * 24 + (8 * n + c + 1))

                done = 0
                for st_in, st_out, kc in S[name]:
                    if done == 0:
                        plain(st_in, 0, 0, range(KD), hh, hl, L, 0, before=chunk_ready)
                        norm(S[name + "norm"], n, L)
                        for k in range(1, 4):
                            plain(st_in, k, k, range(KD), hh, hl, L, 0)
                    with pe.Fori(1 if done == 0 else 0, st_in.steps) as i:
                        for k in range(4):
                            plain(st_in, k, k, range(KD), hh, hl, L, i)
                    done += kc
                    wait_apart(pe, a_ready, L * 44 + (22 * (n // 2) + done))
                    with pe.Fori(0, 2) as i:
                        for k in range(4):
                            plain(st_out, k, k, range(kc), ah, al, L, i)

            pe.wait_ge(x_loaded, X_LOADS * 16)
            for c in range(KD):
                if c >= 4:
                    pe.wait_ge(freed[c % 4], c // 4)
                for b in range(5):
                    rows_ = P if b < 4 else NS
                    out = ps[c % 4][:, 0, b * P:(b + 1) * P] if b < 4 else ps[c % 4][:, 1, 0:NS]
                    last = pe.transpose(out, xin[0:rows_, b, c * P:(c + 1) * P], ident[0:rows_, 0:rows_])
                last.then_inc(filled[c % 4], 1)
            pe.wait_ge(consts_ready, 1)
            pe.wait_ge(in_loaded, IN_LOADS * 16)
            for g in (8, 9):
                pe.wait_ge(freed[g % 4], g // 4)
                for l in range(DEPTH):
                    if g == 8:
                        for t in range(4):
                            last = pe.transpose(ps[0][:, l, t * NR:(t + 1) * NR], rows[:, l, t * P:(t + 1) * P], ident[0:NR, 0:NR])
                    else:
                        last = pe.transpose(ps[1][:, 0, l * 26:(l + 1) * 26], rowsg[:, l, :], ident[0:26, 0:26])
                last.then_inc(filled[g % 4], 1)
            for g in (10, 11):
                pe.wait_ge(freed[g % 4], g // 4)
                pe.transpose(ps[g % 4][:, 0, 0:P], ident, ident).then_inc(filled[g % 4], 1)

            with pe.Fori(0, DEPTH) as L:
                ffn("ffn1", 0, L)
                fv = S["fv"]
                pe.wait_ge(wf_ready, L + 2)
                wait_psum(fv, 0, L)
                for k in range(KD):
                    pe.wait_ge(h_ready, L * 24 + (8 + k + 1))
                    for half in range(2):
                        span = slice(half * HF, half * HF + HF)
                        out = ps[fv.slot(0)][:, half, 0:HF]
                        wh, wl = wfh[:, k * F_W:k * F_W + P], wfl[:, k * F_W:k * F_W + P]
                        pe.matmul(out, wh, hh[:, k, span], start=(k == 0), stop=False)
                        pe.matmul(out, wh, hl[:, k, span], start=False, stop=False)
                        last = pe.matmul(out, wl, hh[:, k, span], start=False, stop=(k == KD - 1))
                last.then_inc(filled[fv.slot(0)], 1)
                norm(S["mixnorm"], 1, L)

                def values(u):
                    wait_weights(fv, 2 * u + 1, L)
                    for b in range(5):
                        k_ = (1, 4)[u] + (b == 4)
                        if b in (0, 4):
                            wait_psum(fv, k_, L)
                        out = ps[fv.slot(k_)][:, b // 2 % 2, (b % 2) * 256:(b % 2) * 256 + 256]
                        tok = slice(b * P, b * P + P) if b < 4 else slice(N - P, N)
                        for k in range(KD):
                            rh = whi[:, :, k * P:(k + 1) * P]
                            rl = wlo[:, :, k * P:(k + 1) * P]
                            pe.matmul(out, hh[:, k, tok], rh, start=(k == 0), stop=False)
                            pe.matmul(out, hl[:, k, tok], rh, start=False, stop=False)
                            last = pe.matmul(out, hh[:, k, tok], rl, start=False, stop=(k == KD - 1))
                        if b in (3, 4):
                            last.then_inc(filled[fv.slot(k_)], 1)

                values(0)
                pe.wait_ge(lfp_ready, L + 1)
                wait_psum(fv, 3, L)
                for g in range(NPG):
                    last = pe.transpose(ps[fv.slot(3)][:, 0, g * P:(g + 1) * P], lfp[:, g, :], ident)
                pe.wait_ge(rstd_ready, L + 1)
                for b in range(5):
                    tok = slice(b * P, b * P + P) if b < 4 else slice(N - P, N)
                    out = ps[fv.slot(3)][:, 1, b * P:(b + 1) * P] if b < 4 else ps[fv.slot(3)][:, 0, 2 * P:3 * P]
                    last = pe.transpose(out, tmp[6][:, tok], ident)
                last.then_inc(filled[fv.slot(3)], 1)
                values(1)
                pe.wait_ge(logf_ready, L + 1)
                wait_psum(fv, 6, L)
                pe.matmul(ps[fv.slot(6)][:, 0, 0:NS], const[0:H, C_REP:C_REP + P], lf[0:H, SEQ:N], start=True, stop=True)\
                    .then_inc(filled[fv.slot(6)], 1)
                wait_apart(pe, freed[fv.slot(7)], fv.turn(7, L))
                for b in range(5):
                    tok = slice(b * P, b * P + P) if b < 4 else slice(N - P, N)
                    last = pe.transpose(ps[fv.slot(7)][:, 0, b * H:(b + 1) * H], lf[0:H, tok], ident[0:H, 0:H])
                last.then_inc(filled[fv.slot(7)], 1)

                pr = S["pair"]
                with pe.Fori(0, PAIRS) as p:
                    it = L * PAIRS + p
                    plain(pr, 0, 0, range(KD), hh, hl, L, p)
                    plain(pr, 1, 1, range(KD), hh, hl, L, p)
                    plain(pr, 2, 2, range(KD), hh, hl, L, p)
                    for k in (3, 4):
                        pe.wait_ge(qk_squared, it * 2 + (k - 2))
                        wait_psum(pr, k, L, p)
                        for half in range(2):
                            last = pe.matmul(ps[pr.slot(k)][:, half, 0:HF], bones, tmp[k - 3][:, half * HF:half * HF + HF], start=True, stop=True)
                        last.then_inc(filled[pr.slot(k)], 1)
                    plain(pr, 5, 3, range(KD), hh, hl, L, p)
                    plain(pr, 6, 4, range(KD), hh, hl, L, p)
                    pe.wait_ge(kv_loaded, it * 512 + 256)
                    for k in (7, 8):
                        wait_psum(pr, k, L, p)
                        for g in range(8):
                            last = pe.transpose(ps[pr.slot(k)][:, g // 4, (g % 4) * P:(g % 4 + 1) * P], kv[:, (k - 7) * 8 + g, :], ident)
                        last.then_inc(filled[pr.slot(k)], 1)
                    pe.wait_ge(qk_ready, it + 1)
                    for e in range(2):
                        for qb in range(QB):
                            k = 9 + 2 * e + qb // 2
                            if qb % 2 == 0:
                                wait_psum(pr, k, L, p)
                            n = (qb + 1) * P
                            out = ps[pr.slot(k)][:, qb % 2, :]
                            hs = slice(HD * e, HD * (e + 1))
                            qs = slice(qb * P, (qb + 1) * P)
                            pe.matmul(out[:, 0:n], qp[hs, qs], kp[hs, 0:n], start=True, stop=False)
                            pe.matmul(out[:, 0:n], cq[e][:, qs], ck[:, 0:n], start=False, stop=False)
                            last = pe.matmul(out[:, qb * P:n], identb[:], maskd[:], start=False, stop=True)
                            if qb % 2:
                                last.then_inc(filled[pr.slot(k)], 1)
                    wait_psum(pr, 13, L, p)
                    for k in (7, 8):
                        pe.wait_ge(freed[pr.slot(k)], pr.turn(k, L, p) + 1)
                    out = ps[pr.slot(13)][:, 0, :]
                    pe.matmul(out[:, 0:3 * P], lhss[:], rhss[:], start=True, stop=False, skip_group_check=True)
                    pe.matmul(out[:, PAST:PAST + P], identb[:], masks[:], start=False, stop=False, skip_group_check=True)
                    for q in qeo:
                        pe.matmul(out[:, PAST:PAST + P], q[:], kp[:, N - P:N], start=False, stop=False, skip_group_check=True)
                    for s in range(SB):
                        quad = slice(32 * (s // 2), 32 * (s // 2) + 32)
                        pe.matmul(out[quad, 0:PAST], qeo[s % 2][:, quad], kpt[:, s * PAST:(s + 1) * PAST],
                                  start=False, stop=(s == SB - 1), skip_group_check=True, tile_position=(0, quad.start))
                    pe.transpose(ps[pr.slot(13)][:, 0, 3 * P:4 * P], kp[:, N - P:N], ident)
                    for b in range(4):
                        last = pe.transpose(ps[pr.slot(13)][:, 1, b * P:(b + 1) * P], kp[:, b * P:(b + 1) * P], ident)
                    last.then_inc(filled[pr.slot(13)], 1)
                    plain(pr, 14, 5, range(KD), hh, hl, L, p)
                    pe.wait_ge(xc_ready, it + 1)
                    pe.wait_ge(wab_loaded, it * 64 + 64)
                    for k in (15, 16):
                        wait_psum(pr, k, L, p)
                        for half in range(2):
                            last = pe.matmul(ps[pr.slot(k)][:, half, 0:XB // 2], wab[:, k - 15, :],
                                             tmp[3][:, half * (XB // 2):(half + 1) * (XB // 2)], start=True, stop=True)
                        last.then_inc(filled[pr.slot(k)], 1)

                    offs = [0, P, 3 * P, 6 * P]
                    koffs = [0, 4 * P, 7 * P, 9 * P]

                    def transposed(e, k0):
                        pe.wait_ge(prob_ready, it * 3 + (e + 1))
                        for kb in range(QB):
                            k = k0 + kb // 2
                            if kb % 2 == 0:
                                wait_psum(pr, k, L, p)
                            for qb in range(kb, QB):
                                last = pe.transpose(ps[pr.slot(k)][:, kb % 2, (qb - kb) * P:(qb - kb + 1) * P],
                                                    prob[e][:, offs[qb] + kb * P:offs[qb] + (kb + 1) * P], ident)
                            if kb % 2:
                                last.then_inc(filled[pr.slot(k)], 1)

                    def weighted(e):
                        k = (18, 23)[e]
                        pe.wait_ge(freed[pr.slot(k)], pr.turn(k, L, p) + 1)
                        for kb in range(QB):
                            last = pe.matmul(ps[pr.slot(21)][HD * e:HD * (e + 1), 0, kb * P:SEQ], vp[:, kb, HD * e:HD * (e + 1)],
                                             probt[:, koffs[kb]:koffs[kb] + (QB - kb) * P], start=(kb == 0), stop=(kb == QB - 1),
                                             skip_group_check=True)
                        return last

                    transposed(0, 17)
                    pe.wait_ge(prob_ready, it * 3 + 3)
                    wait_psum(pr, 19, L, p)
                    for c in range(3):
                        last = pe.transpose(ps[pr.slot(19)][:, 0, c * P:(c + 1) * P], probs[:, c * P:(c + 1) * P], ident)
                    last.then_inc(filled[pr.slot(19)], 1)
                    wait_weights(pr, 6, L, p)
                    wait_psum(pr, 20, L, p)
                    project(pr.slot(20), 6, range(4), hh, hl, stop=False)
                    wait_weights(pr, 7, L, p)
                    project(pr.slot(20), 7, range(4, KD), hh, hl, start=False).then_inc(filled[pr.slot(20)], 1)
                    pe.wait_ge(vp_ready, it + 1)
                    wait_psum(pr, 21, L, p)
                    weighted(0).then_inc(pv_done, 1)
                    transposed(1, 22)
                    pe.wait_ge(freed[pr.slot(19)], pr.turn(19, L, p) + 1)
                    pe.wait_ge(kv_loaded, it * 512 + 512)
                    out = ps[pr.slot(21)][:, 1, :]
                    pe.matmul(out[:, 0:P], vp[:, 4, :], probst[:, 2 * P:3 * P], start=True, stop=False, skip_group_check=True)
                    for s in range(SB):
                        rs = slice(16 * s, 16 * s + 16)
                        for g in range(NPG):
                            pe.matmul(out[:, rs], kv[:, s * NPG + g, :], probst[:, g * P + 16 * s:g * P + 16 * s + 16],
                                      start=False, stop=(s == SB - 1 and g == NPG - 1), skip_group_check=True)
                    weighted(1).then_inc(filled[pr.slot(21)], 1)

                st = S["state"]
                pe.wait_ge(f_ready, L + 1)
                wait_apart(pe, freed[st.slot(0)], st.turn(0, L))
                for t in range(4):
                    last = pe.transpose(ps[st.slot(0)][0:NO, 0, t * P:(t + 1) * P], fout[:, t, :], ident)
                last.then_inc(filled[st.slot(0)], 1)

                mg = S["merge"]
                with pe.Fori(0, mg.steps) as i:
                    for b in range(3):
                        for j in range(2):
                            plain(mg, 4 * b + j, 4 * b + j, range(KD), hh, hl, L, i)
                        pe.wait_ge(o_ready, L * 12 + 4 * (b + 1))
                        for j in range(2, 4):
                            plain(mg, 4 * b + j, 4 * b + j, range(4 * b, 4 * b + 4), oh, ol, L, i)
                with pe.Fori(0, 2) as i:
                    for k in range(4):
                        plain(S["out"], k, k, range(KD), mh, ml, L, i, before=(lambda c: pe.wait_ge(m_ready, L * 8 + (c + 1))) if k == 0 else None)
                ffn("ffn2", 2, L)
                for g in range(plan["tiles_used"], plan["layer_tiles"]):
                    pe.wait_ge(freed[g % 4], L * (plan["layer_tiles"] // 4) + (PRE_TILES + g) // 4)
                    pe.transpose(ps[g % 4][:, 0, 0:P], ident, ident).then_inc(filled[g % 4], 1)

            post = DEPTH * plan["layer_tiles"] + PRE_TILES
            last_st = S["ffn2"][-1][1]
            for k in range(4):
                pe.wait_ge(freed[last_st.slot(k)], last_st.turn(k, DEPTH - 1, 1) + 1)
            for b in range(5):
                g = post + b
                tok = slice(b * P, b * P + P) if b < 4 else slice(N - P, N)
                pe.wait_ge(freed[g % 4], g // 4)
                for c in range(KD):
                    last = pe.transpose(ps[g % 4][:, c // 4, (c % 4) * P:(c % 4 + 1) * P], x[:, c, tok], ident)
                last.then_inc(filled[g % 4], 1)

        @block.scalar
        def _(act):
            def wait_tile(st, k, L, i=0):
                act.wait_ge(filled[st.slot(k)], st.turn(k, L, i) + 1)

            def split_ahead(st, w, k, L, i=0):
                wait_tile(st, k, L, i)
                u, j, rowwise = ahead(st, w)
                base = st.first_unit + u
                slot = base % 2
                act.wait_ge(unit_loaded[slot], L * (plan["layer_units"] // 2 * 32) + i * (st.units // 2 * 32) + (base // 2 + 1) * 32)
                act.activation(split_tile(whi, j, rowwise), raw_tile(slot, j, rowwise), ACT.Copy).then_inc(hi_ready, 1)

            def root(st, L):
                wait_tile(st, 0, L)
                act.activation(two(tmp[6][:, 0:N]), cols(st.slot(0)), ACT.Sqrt, bias=eps[:, 0:1]).then_inc(freed[st.slot(0)], 1)

            def update(st, q0, L, gain_row=None, gain_at=0):
                with act.Fori(0, 2) as i:
                    for k in range(4):
                        split_ahead(st, k, k, L, i)
                        if q0 is None:
                            continue
                        act.wait_ge(freed[st.slot(k)], st.turn(k, L, i) + 1)
                        act.wait_ge(sq_added, L * 24 + i * 4 + (q0 + k - 1))
                        act.activation(tmp[2 + k % 2][:, 0:N], chunk(x, i * 4 + k), ACT.Square).then_inc(sq_ready, 1)
                        if gain_row is not None:
                            act.activation(chunk(hh, i * 4 + k), chunk(x, i * 4 + k), ACT.Copy,
                                           scale=norm_gain(gain_row, i * 4 + (gain_at + k))).then_inc(hh_ready, 1)

            def ffn(name, n, L):
                root(S[name + "norm"], L)
                done = 0
                for part, (st_in, st_out, kc) in enumerate(S[name]):
                    with act.Fori(0, st_in.steps) as i:
                        for k in range(4):
                            split_ahead(st_in, k, k, L, i)
                            if k < 2:
                                act.wait_ge(freed[st_in.slot(k)], st_in.turn(k, L, i) + 1)
                                act.activation(tmp[k][:, 0:N], tmp[k][:, 0:N], ACT.Silu).then_inc(silu_ready, 1)
                    if part < 2:
                        update(st_out, None, L)
                    elif n == 0:
                        update(st_out, 8, L, L, 8)
                    else:
                        update(st_out, 24, L, L + 1)
                    done += kc

            act.wait_ge(pre_done, 1)
            for c in range(KD):
                act.wait_ge(filled[c % 4], c // 4 + 1)
                act.activation(x[:, c, 0:SEQ], ps[c % 4][:, 0, :], ACT.Copy)
                act.activation(x[:, c, SEQ:N], ps[c % 4][:, 1, 0:NS], ACT.Copy).then_inc(freed[c % 4], 1)
                act.drain()
                if c >= 2:
                    act.wait_ge(sq_added, c - 1)
                act.activation(tmp[2 + c % 2][:, 0:N], x[:, c, :], ACT.Square).then_inc(sq_ready, 1)
            act.wait_ge(filled[0], 3)
            act.activation(par_all[:, :, :], ps[0][:, :, 0:4 * NR], ACT.Copy).then_inc(freed[0], 1)
            act.wait_ge(filled[1], 3)
            act.activation(gains[:, 0:DEPTH, :].rearrange("p l n -> p (l n)"), ps[1][:, 0, 0:52], ACT.Copy).then_inc(freed[1], 1)
            for g in (10, 11):
                act.wait_ge(filled[g % 4], g // 4 + 1)
                act.activation(small[:, 60:61], ps[g % 4][:, 0, 0:1], ACT.Copy).then_inc(freed[g % 4], 1)
                act.drain()
            act.drain()
            def first_weights(j):
                act.wait_ge(unit_loaded[0], 32)
                act.activation(split_tile(whi, j), raw_tile(0, j), ACT.Copy).then_inc(hi_ready, 1)

            first_weights(0)
            for c in range(KD):
                act.activation(hh[:, c, :], x[:, c, :], ACT.Copy, scale=gains[:, 0, c:c + 1]).then_inc(hh_ready, 1)
            first_weights(1)
            act.wait_ge(pre_done, 2)
            act.activation(spt[1][:], spt[0][:], ACT.Exp, scale=-1.0).then_inc(consts_ready, 1)

            with act.Fori(0, DEPTH) as L:
                act.wait_ge(wf_loaded, L * 32 + 32)
                act.activation(wfh[:, 0:KD * F_W], wfr[:, :, :].rearrange("p k c -> p (k c)"), ACT.Copy).then_inc(wf_hi, 1)
                ffn("ffn1", 0, L)
                root(S["mixnorm"], L)
                fv = S["fv"]
                act.wait_ge(absz_ready, L + 1)
                act.activation(tmp[3][0:F_W, 0:N], tmp[2][0:F_W, 0:N], ACT.Exp, scale=-1.0).then_inc(expz_ready, 1)
                split_ahead(fv, 0, 2, L)
                split_ahead(fv, 1, 2, L)
                wait_tile(fv, 3, L)
                act.activation(cs[:, 0:PAST], ps[fv.slot(3)][:, 0, 0:PAST], ACT.Copy)
                act.activation(small[:, 11:15], ps[fv.slot(3)][:, 1, :].rearrange("p (b n) -> p b n", n=P)[:, :, 0], ACT.Copy)
                act.activation(small[:, 15:16], ps[fv.slot(3)][:, 0, 2 * P:2 * P + 1], ACT.Copy).then_inc(freed[fv.slot(3)], 1)
                act.drain()
                for u in range(2):
                    k = (1, 4)[u]
                    wait_tile(fv, k, L)
                    if u:
                        split_ahead(fv, 2, 5, L)
                        split_ahead(fv, 3, 5, L)
                    for b in range(5):
                        if b == 4:
                            wait_tile(fv, k + 1, L)
                        ins = act.activation(vtok[:, b, u * 256:(u + 1) * 256],
                                             ps[fv.slot(k + b // 4)][:, b // 2 % 2, b % 2 * 256:b % 2 * 256 + 256], ACT.Copy,
                                             scale=small[:, 11 + b:12 + b])
                        if b >= 3:
                            ins.then_inc(freed[fv.slot(k + b // 4)], 1)
                wait_tile(fv, 7, L)
                act.activation(lfo[:, :, :].rearrange("p b h -> p (b h)"), ps[fv.slot(7)][:, 0, 0:5 * H], ACT.Copy)\
                    .then_inc(freed[fv.slot(7)], 1)

                pr = S["pair"]
                with act.Fori(0, PAIRS) as p:
                    it = L * PAIRS + p

                    def free(k):
                        return freed[pr.slot(k)]

                    for k in (0, 1):
                        split_ahead(pr, k, k, L, p)
                        act.wait_ge(free(k), pr.turn(k, L, p) + 1)
                        act.activation(tmp[k][:, 0:N], (qp, kp)[k][:], ACT.Square).then_inc(qk_squared, 1)
                    split_ahead(pr, 2, 2, L, p)
                    for k in (3, 4):
                        wait_tile(pr, k, L, p)
                        act.activation(two(tmp[k - 3][:, 0:N]), cols(pr.slot(k)), ACT.Sqrt, bias=eps[:, 0:1]).then_inc(free(k), 1)
                    split_ahead(pr, 3, 5, L, p)
                    act.activation(two(chunk(o, p + 4)), cols(pr.slot(5)), ACT.Copy).then_inc(free(5), 1)
                    split_ahead(pr, 4, 6, L, p)
                    act.activation(two(tmp[5][:, 0:N]), cols(pr.slot(6)), ACT.Copy).then_inc(free(6), 1)
                    for k in (7, 8):
                        wait_tile(pr, k, L, p)
                        act.activation(kpt[:, (k - 7) * 1024:(k - 6) * 1024], ps[pr.slot(k)][:, :, :].rearrange("p b n -> p (b n)"), ACT.Copy)\
                            .then_inc(free(k), 1)

                    for e in range(2):
                        act.wait_ge(max_ready, it * 3 + (e + 1))
                        for qb in range(QB):
                            k = 9 + 2 * e + qb // 2
                            n = (qb + 1) * P
                            off = (0, P, 3 * P, 6 * P)[qb]
                            ins = act.activation(prob[e][:, off:off + n], ps[pr.slot(k)][:, qb % 2, 0:n], ACT.Exp,
                                                 bias=small[:, 4 * e + qb:4 * e + qb + 1], accum_out=small[:, 16 + 4 * e + qb:17 + 4 * e + qb])
                            if qb % 2:
                                ins.then_inc(free(k), 1)
                    act.wait_ge(max_ready, it * 3 + 3)
                    act.activation(probs[:], ps[pr.slot(13)][:, 0, 0:3 * P], ACT.Exp, bias=small[:, 8:9], accum_out=small[:, 24:25])\
                        .then_inc(exp_ready, 1)
                    act.activation(kout[:, 4, :], ps[pr.slot(13)][:, 0, 3 * P:4 * P], ACT.Copy)
                    act.activation(kout[:, 0:4, :].rearrange("p b n -> p (b n)"), ps[pr.slot(13)][:, 1, :], ACT.Copy).then_inc(free(13), 1)
                    split_ahead(pr, 5, 14, L, p)
                    for k in (15, 16):
                        wait_tile(pr, k, L, p)
                        act.activation(tmp[(4, 1)[k - 15]][:, 0:XB].rearrange("p (b n) -> p b n", b=2), ps[pr.slot(k)][:, :, 0:XB // 2],
                                       ACT.Sigmoid, bias=prow[:, R_BA + (k - 15):R_BA + 1 + (k - 15)]).then_inc(free(k), 1)
                    act.wait_ge(free(16), pr.turn(16, L, p) + 1)
                    act.wait_ge(free(14), pr.turn(14, L, p) + 1)
                    act.activation(tmp[0][:, 0:XB], tmp[4][:, 0:XB], ACT.Exp, scale=nbias[:, 0:1])
                    act.activation(tmp[5][:, 0:XB], tmp[4][:, 0:XB], ACT.Tanh, scale=nbias[:, 1:2])
                    act.drain()
                    act.activation(tmp[4][:, 0:XB], tmp[0][:, 0:XB], ACT.Square).then_inc(gates_ready, 1)

                    def copy_pt(k0):
                        for kb in range(QB):
                            k = k0 + kb // 2
                            if kb % 2 == 0:
                                wait_tile(pr, k, L, p)
                            w = (QB - kb) * P
                            off = (0, 4 * P, 7 * P, 9 * P)[kb]
                            ins = act.activation(probt[:, off:off + w], ps[pr.slot(k)][:, kb % 2, 0:w], ACT.Copy)
                            if kb == 1:
                                ins.then_inc(free(k), 1)
                        ins.then_inc(free(k0 + 1), 1)

                    copy_pt(17)
                    act.wait_ge(by_ready, it + 1)
                    wait_tile(pr, 19, L, p)
                    act.activation(probst[:], ps[pr.slot(19)][:, 0, 0:3 * P], ACT.Copy).then_inc(free(19), 1)
                    act.activation(chunk(o, p + 4), chunk(o, p + 4), ACT.Gelu_apprx_tanh).then_inc(gelu_ready, 1)
                    act.wait_ge(root_in, it + 1)
                    act.activation(tmp[5][:, 0:XB], tmp[5][:, 0:XB], ACT.Sqrt, bias=eps[:, 1:2]).then_inc(root_ready, 1)
                    split_ahead(pr, 6, 20, L, p)
                    split_ahead(pr, 7, 20, L, p)
                    act.wait_ge(pv_done, it + 1)
                    copy_pt(22)
                    wait_tile(pr, 21, L, p)
                    op = o[:, bass.ds(p, 1), :].rearrange("p a n -> p (a n)")
                    act.activation(op[:, 0:SEQ], ps[pr.slot(21)][:, 0, :], ACT.Copy)
                    for e in range(2):
                        hs = slice(HD * e, HD * (e + 1))
                        src = ps[pr.slot(21)][hs, 1, 0:P].rearrange("p (s c) -> p s c", c=16)[:, :, ST * e:ST * (e + 1)]
                        dst = o[hs, bass.ds(p, 1), SEQ:N].rearrange("p a (s t) -> p (a s) t", t=ST)
                        ins = act.activation(dst, src, ACT.Copy)
                    ins.then_inc(free(21), 1)
                    act.wait_ge(k_stored, it * 32 + 32)

                act.drain()
                st = S["state"]
                wait_tile(st, 0, L)
                act.wait_ge(f_ready, L + 1)
                for c in range(12):
                    act.activation(oh[:, c, :], o[:, c, :], ACT.Copy).then_inc(oh_ready, 1)
                act.activation(frow[:, :], ps[st.slot(0)][0:NO, 0, :], ACT.Copy).then_inc(freed[st.slot(0)], 1)
                mg = S["merge"]
                with act.Fori(0, mg.steps) as i:
                    for b in range(3):
                        for j in range(4):
                            k = 4 * b + j
                            split_ahead(mg, k, k, L, i)
                            if j < 2:
                                act.wait_ge(freed[mg.slot(k)], mg.turn(k, L, i) + 1)
                                act.activation(tmp[j][:, 0:N], tmp[j][:, 0:N], ACT.Sigmoid).then_inc(gate_ready, 1)
                update(S["out"], 16, L, L, 16)
                ffn("ffn2", 2, L)
                act.wait_ge(v_stored, L * 32 + 32)
                act.wait_ge(lf_stored, L * 32 + 32)
                act.wait_ge(f_stored, L * 96 + 96)
                for g in range(plan["tiles_used"], plan["layer_tiles"]):
                    act.wait_ge(filled[g % 4], L * (plan["layer_tiles"] // 4) + (PRE_TILES + g) // 4 + 1)
                    act.activation(small[:, 60:61], ps[g % 4][:, 0, 0:1], ACT.Copy).then_inc(freed[g % 4], 1)
                    act.drain()

            post = DEPTH * plan["layer_tiles"] + PRE_TILES
            for b in range(5):
                g = post + b
                act.wait_ge(filled[g % 4], g // 4 + 1)
                act.activation(yout[:, b, :], ps[g % 4][:, :, :].rearrange("p b n -> p (b n)"), ACT.Copy).then_inc(freed[g % 4], 1)

        @block.vector
        def _(dve):
            def wait_tile(st, k, L, i=0):
                dve.wait_ge(filled[st.slot(k)], st.turn(k, L, i) + 1)

            def split_ahead(st, w, L, i=0):
                u, j, rowwise = ahead(st, w)
                slot = (st.first_unit + u) % 2
                dve.wait_ge(hi_ready, st.unit(0, L, i) * 2 + (w + 3))
                dve.tensor_tensor(split_tile(wlo, j, rowwise), raw_tile(slot, j, rowwise), split_tile(whi, j, rowwise).bitcast(F32),
                                  ALU.subtract).then_inc(lo_ready, 1)

            def rstd(st, L):
                dve.wait_ge(freed[st.slot(0)], st.turn(0, L) + 1)
                dve.reciprocal(tmp[6][:, 0:N], tmp[6][:, 0:N])
                return dve.drain()

            def update(st, L, half, h0=None, gain_row=None, gain_at=0):
                with dve.Fori(0, 2) as i:
                    for k in range(4):
                        split_ahead(st, k, L, i)
                        wait_tile(st, k, L, i)
                        xm = chunk(x, i * 4 + k)
                        dve.scalar_tensor_tensor(out=two(xm), in0=cols(st.slot(k)), scalar=half, in1=two(xm), op0=ALU.mult, op1=ALU.add)\
                            .then_inc(freed[st.slot(k)], 1)
                        if gain_row is not None:
                            dve.wait_ge(hh_ready, L * 24 + i * 4 + (h0 + k + 1))
                            dve.scalar_tensor_tensor(out=chunk(hl, i * 4 + k), in0=xm, scalar=norm_gain(gain_row, i * 4 + (gain_at + k)),
                                                     in1=chunk(hh, i * 4 + k).bitcast(F32), op0=ALU.mult, op1=ALU.subtract)\
                                .then_inc(h_ready, 1)

            def ffn(name, n, L):
                rstd(S[name + "norm"], L)
                done = 0
                for part, (st_in, st_out, kc) in enumerate(S[name]):
                    with dve.Fori(0, st_in.steps) as i:
                        for k in range(4):
                            split_ahead(st_in, k, L, i)
                            wait_tile(st_in, k, L, i)
                            pf = tmp[k if k < 2 else 2 + k]
                            dve.tensor_tensor(two(pf[:, 0:N]), two(tmp[6][:, 0:N]), cols(st_in.slot(k)), ALU.mult)\
                                .then_inc(freed[st_in.slot(k)], 1)
                            if k < 2:
                                continue
                            j = i * 2 + (k - 2)
                            dve.drain()
                            dve.wait_ge(silu_ready, L * 44 + i * 2 + (22 * (n // 2) + done + k - 1))
                            dve.tensor_tensor(pf[:, 0:N], pf[:, 0:N], tmp[k - 2][:, 0:N], ALU.mult)
                            dve.drain()
                            dve.tensor_copy(chunk(ah, j), pf[:, 0:N])
                            dve.drain()
                            dve.tensor_tensor(chunk(al, j), pf[:, 0:N], chunk(ah, j).bitcast(F32), ALU.subtract).then_inc(a_ready, 1)
                    if part == 2:
                        update(st_out, L, 0.5, *((8, L, 8) if n == 0 else (24, L + 1)))
                    else:
                        update(st_out, L, 0.5)
                    done += kc

            def log1p(t, r, s, s2, acc, between=None):
                dve.tensor_scalar(r, t, 2.0, None, ALU.add)
                dve.drain()
                dve.reciprocal(r, r)
                dve.drain()
                dve.tensor_tensor(s, t, r, ALU.mult)
                dve.drain()
                dve.tensor_tensor(s2, s, s, ALU.mult)
                dve.drain()
                dve.tensor_scalar(acc, s2, 1.0 / 17, None, ALU.mult)
                for k in range(15, 1, -2):
                    if k == 7 and between:
                        between()
                    dve.drain()
                    dve.scalar_tensor_tensor(out=acc, in0=acc, scalar=1.0 / k, in1=s2, op0=ALU.add, op1=ALU.mult)
                dve.drain()
                dve.scalar_tensor_tensor(out=acc, in0=acc, scalar=1.0, in1=s, op0=ALU.add, op1=ALU.mult)
                dve.drain()
                dve.tensor_scalar(acc, acc, 2.0, None, ALU.mult)
                dve.drain()

            dve.memset(eps[:, 0:1], EPS)
            dve.memset(eps[:, 1:2], 2e-35)
            dve.memset(gains[:, DEPTH, :], 0.0)
            dve.memset(wfh[:, KD * F_W:].bitcast(F32), 0.0)
            dve.memset(wfl[:, KD * F_W:].bitcast(F32), 0.0)
            dve.memset(wab[:, :, :], 0.0)
            dve.memset(small[:], 0.0).then_inc(pre_done, 1)
            dve.memset(wlo[:, 0, 0:1].bitcast(F32), 0.0).then_inc(lo_ready, AHEAD)
            dve.memset(wlo[:, 0, 1:2].bitcast(F32), 0.0).then_inc(wf_ready, 1)
            dve.wait_ge(x_loaded, X_LOADS * 16)
            dve.wait_ge(in_loaded, IN_LOADS * 16)
            dve.tensor_copy(identb[:], ident)
            dve.tensor_copy(maskd[:], cmask[:, 0:P])
            dve.tensor_copy(masks[:], cmask[:, P:2 * P]).then_inc(consts_ready, 1)
            def first_weights(j):
                dve.wait_ge(hi_ready, j + 1)
                dve.tensor_tensor(split_tile(wlo, j), raw_tile(0, j), split_tile(whi, j).bitcast(F32), ALU.subtract).then_inc(lo_ready, 1)

            dve.wait_ge(freed[1], 3)
            first_weights(0)
            for c in range(KD):
                dve.wait_ge(hh_ready, c + 1)
                dve.scalar_tensor_tensor(out=hl[:, c, :], in0=x[:, c, :], scalar=gains[:, 0, c:c + 1], in1=hh[:, c, :].bitcast(F32),
                                         op0=ALU.mult, op1=ALU.subtract).then_inc(h_ready, 1)
            first_weights(1)
            dve.wait_ge(freed[0], 3)
            lam = par_all[:, :, :].rearrange("p l (t r) -> p l t r", r=NR)[:, :, :, R_LAM]
            dve.scalar_tensor_tensor(out=spt[0][:], in0=lam, scalar=-1.0, in1=lam, op0=ALU.mult, op1=ALU.max).then_inc(pre_done, 1)
            dve.wait_ge(consts_ready, 2)
            log1p(spt[1][:], spt[2][:], spt[3][:], spt[4][:], spt[2][:])
            dve.tensor_scalar(spt[3][:], lam, -1.0, 0.0, ALU.mult, ALU.max)
            dve.drain()
            dve.tensor_tensor(spt[4][:], spt[3][:], spt[2][:], ALU.add)
            dve.drain()
            dve.tensor_scalar(decay[:, :, 0, :], spt[4][:], -8.0, None, ALU.mult)
            dve.tensor_scalar(decay[:, :, 1, :], spt[4][:], 8.0, None, ALU.mult)

            with dve.Fori(0, DEPTH) as L:
                dve.drain()
                dve.tensor_copy(gain[:], gains[:, bass.ds(L, 1), :].rearrange("p l n -> p (l n)"))
                dve.tensor_copy(bf[:], bfor[:, bass.ds(L, 1)])
                dve.tensor_copy(dk[:, :, :].rearrange("p a t -> p (a t)"), decay[:, bass.ds(L, 1), :, :].rearrange("p l a t -> p (l a t)"))
                dve.wait_ge(wf_hi, L + 1)
                dve.tensor_tensor(wfl[:, 0:KD * F_W], wfr[:, :, :].rearrange("p k c -> p (k c)"), wfh[:, 0:KD * F_W].bitcast(F32),
                                  ALU.subtract).then_inc(wf_ready, 1)
                dve.drain()
                dve.tensor_scalar(gain[:, 24:25], gain[:, 24:25], HD ** -0.5, None, ALU.mult)
                ffn("ffn1", 0, L)
                rstd(S["mixnorm"], L).then_inc(rstd_ready, 1)

                fv = S["fv"]
                dve.memset(cp[:], 0.0)
                dve.memset(rhss[0:NS, PAST:PAST + NS], 0.0)
                dve.memset(rhss[NS:P, :], 1.0)
                for q in qeo:
                    dve.memset(q[:], 0.0)
                dve.wait_ge(lfp_loaded, L * (SB * NPG * 16) + SB * NPG * 16)
                dve.tensor_copy(lfp[:, :, NS:2 * NS], lfp[:, :, 0:NS]).then_inc(lfp_ready, 1)
                z, az, ez = tmp[0][0:F_W, 0:N], tmp[2][0:F_W, 0:N], tmp[3][0:F_W, 0:N]
                wait_tile(fv, 0, L)
                dve.tensor_tensor(two(z), ps[fv.slot(0)][0:F_W, :, 0:HF], two(tmp[6][0:F_W, 0:N]), ALU.mult).then_inc(freed[fv.slot(0)], 1)
                dve.drain()
                dve.tensor_scalar(z, z, bf[:, 0:1], None, ALU.add)
                dve.drain()
                dve.scalar_tensor_tensor(out=az, in0=z, scalar=-1.0, in1=z, op0=ALU.mult, op1=ALU.max).then_inc(absz_ready, 1)
                dve.wait_ge(expz_ready, L + 1)
                t1, t2, t3 = tmp[1][0:F_W, 0:N], tmp[4][0:F_W, 0:N], tmp[5][0:F_W, 0:N]

                def splits():
                    split_ahead(fv, 0, L)
                    split_ahead(fv, 1, L)

                log1p(ez, t1, t2, t3, az, between=splits)
                dve.scalar_tensor_tensor(out=lf[:], in0=z, scalar=0.0, in1=az, op0=ALU.min, op1=ALU.subtract).then_inc(logf_ready, 1)
                dve.drain()
                c0, c1 = tmp[0][0:F_W, 0:SEQ], tmp[1][0:F_W, 0:SEQ]
                mid = tmp[2][0:F_W, 0:SEQ // 2].bitcast(BF16)
                dve.memset(kpt[:, 0:SEQ], 1.0)
                dve.drain()
                dve.tensor_tensor_scan(c0, kpt[0:F_W, 0:SEQ], lf[:, 0:SEQ], 0.0, ALU.mult, ALU.add)
                dve.drain()
                dve.tensor_copy(cp[0:F_W, :], c0)
                dve.drain()
                dve.tensor_tensor(c1, c0, cp[0:F_W, :], ALU.subtract)
                dve.drain()
                dve.tensor_copy(mid, c1)
                dve.drain()
                dve.tensor_copy(cp[32:32 + F_W, :], mid)
                dve.tensor_tensor(cp[64:64 + F_W, :], c1, mid, ALU.subtract)
                dve.drain()
                dve.tensor_scalar(ck[:], cp[:], const[0:96, C_M12:C_M12 + 1], const[0:96, C_M12 + 1:C_M12 + 2], ALU.mult, ALU.add)
                split_ahead(fv, 2, L)
                split_ahead(fv, 3, L)
                wait_tile(fv, 6, L)
                dve.tensor_tensor(tmp[3][:, 0:NS], ps[fv.slot(6)][:, 0, 0:NS], const[:, C_MREP:C_MREP + NS], ALU.mult)\
                    .then_inc(freed[fv.slot(6)], 1)
                dve.drain()
                dve.tensor_reduce(cs[:, PAST:PAST + ST], tmp[3][:, 0:NS].rearrange("p (s t) -> p t s", t=ST), AX.X, ALU.add)
                dve.drain()
                dve.wait_ge(freed[fv.slot(3)], fv.turn(3, L) + 1)
                dve.tensor_tensor_scan(cs[:], kpt[:, 0:PAST + ST], cs[:], 0.0, ALU.mult, ALU.add)
                dve.drain()
                dve.tensor_scalar(rhss[0:NS, 0:PAST], cs[0:NS, 0:PAST], -1.0, None, ALU.mult)
                for s in range(SB):
                    at = PAST + NS + s * ST
                    dve.tensor_scalar(rhss[0:NS, at:at + ST], cs[0:NS, PAST:PAST + ST], -1.0, None, ALU.mult)

                pr = S["pair"]
                with dve.Fori(0, PAIRS) as p:
                    it = L * PAIRS + p

                    def free(k):
                        return freed[pr.slot(k)]

                    dve.tensor_copy(prow[:], par_all[:, bass.ds(L, 1), bass.ds(p * NR, NR)].rearrange("p l n -> p (l n)"))
                    dve.tensor_copy(nbias[:], dk[:, :, bass.ds(p, 1)].rearrange("p a t -> p (a t)"))
                    for e in range(2):
                        at = (p * 2 + e) * 2 + C_SEL
                        dve.tensor_scalar(cq[e][:], cp[:], const[0:96, bass.ds(at, 1)], const[0:96, bass.ds(at + 1, 1)], ALU.mult, ALU.add)
                    dve.tensor_copy(lhss[0:NS, :], const[0:NS, bass.ds(p * P + C_IND, P)])
                    dve.tensor_tensor(lhss[NS:P, :].rearrange("p (a q) -> p a q", q=ST),
                                      const[NS:P, bass.ds(p * P + C_IND, P)].rearrange("p (a q) -> p a q", q=ST),
                                      cs[NS:P, PAST:PAST + ST].rearrange("p (a q) -> p a q", a=1).to_broadcast([NS, 16, ST]), ALU.mult)
                    for k, dst in ((0, qp), (1, kp)):
                        split_ahead(pr, k, L, p)
                        wait_tile(pr, k, L, p)
                        dve.tensor_tensor(two(dst[:]), cols(pr.slot(k)), two(tmp[6][:, 0:N]), ALU.mult).then_inc(free(k), 1)
                    split_ahead(pr, 2, L, p)
                    wait_tile(pr, 2, L, p)
                    u = tmp[2]
                    bx, norm = ps[pr.slot(2)], tmp[6]
                    dve.tensor_tensor(u[:, HB_:HB_ + HF], bx[:, 0, 0:HF], norm[:, 0:HF], ALU.mult)
                    dve.tensor_tensor(u[:, HB_ + HF:HB_ + SEQ], bx[:, 1, 0:SEQ - HF], norm[:, HF:SEQ], ALU.mult)
                    dve.tensor_tensor(sequences(u, SB0, STEP_B, HB_, ST), bx[:, 1, SEQ - HF:HF].rearrange("p (s t) -> p s t", t=ST),
                                      norm[:, SEQ:N].rearrange("p (s t) -> p s t", t=ST), ALU.mult).then_inc(free(2), 1)
                    dve.memset(u[:, 0:HB_], 0.0)
                    dve.tensor_copy(sequences(u, SB0, STEP_B, 0, HB_), prow[:, R_CS:R_CS + SB * HB_].rearrange("p (s r) -> p s r", r=HB_))
                    dve.drain()
                    for k, dst in ((3, qp), (4, kp)):
                        dve.wait_ge(free(k), pr.turn(k, L, p) + 1)
                        t = tmp[k - 3][:, 0:N]
                        dve.reciprocal(t, t)
                        dve.drain()
                        dve.scalar_tensor_tensor(out=dst[:], in0=dst[:], scalar=gain[:, 21 + k:22 + k], in1=t, op0=ALU.mult, op1=ALU.mult)
                    dve.drain()
                    for par in range(2):
                        for e in range(2):
                            hs = slice(HD * e, HD * (e + 1))
                            dst = qeo[par][hs, :].rearrange("p (a b h q) -> p a b h q", b=2, h=2, q=ST)[:, :, par, e, :]
                            src = qp[hs, SEQ:N].rearrange("p (a b q) -> p a b q", b=2, q=ST)[:, :, par, :]
                            ins = dve.tensor_copy(dst, src)
                    ins.then_inc(qk_ready, 1)

                    def taps(out, u, n, w0, kw, bias):
                        if bias is None:
                            dve.tensor_scalar(out[:, 0:n], u[:, 0:n], prow[:, w0:w0 + 1], None, ALU.mult)
                        else:
                            dve.tensor_scalar(out[:, 0:n], u[:, 0:n], prow[:, w0:w0 + 1], prow[:, bias:bias + 1], ALU.mult, ALU.add)
                        for j in range(1, kw):
                            dve.drain()
                            ins = dve.scalar_tensor_tensor(out=out[:, 0:n], in0=u[:, j:j + n], scalar=prow[:, w0 + j:w0 + j + 1],
                                                           in1=out[:, 0:n], op0=ALU.mult, op1=ALU.add)
                        return ins

                    split_ahead(pr, 3, L, p)
                    taps(tmp[3], u, XB, R_CW, CONV_B, R_CB).then_inc(xc_ready, 1)
                    dve.tensor_copy(fcol[:, O_CP:O_CP + HB_], u[:, SEQ:SEQ + HB_])
                    dve.tensor_copy(fcol[:, O_CS:O_CS + SB * HB_].rearrange("p (s r) -> p s r", r=HB_), sequences(u, SB0, STEP_B, ST, HB_))
                    for e in range(2):
                        for qb in range(QB):
                            k = 9 + 2 * e + qb // 2
                            if qb % 2 == 0:
                                wait_tile(pr, k, L, p)
                            dve.tensor_reduce(small[:, 32 + 4 * e + qb:33 + 4 * e + qb], ps[pr.slot(k)][:, qb % 2, 0:(qb + 1) * P], AX.X, ALU.max)
                        dve.drain()
                        dve.tensor_scalar(small[:, 4 * e:4 * e + 4], small[:, 32 + 4 * e:36 + 4 * e], -1.0, None, ALU.mult).then_inc(max_ready, 1)
                    wait_tile(pr, 13, L, p)
                    dve.tensor_reduce(small[:, 9:10], ps[pr.slot(13)][:, 0, 0:3 * P], AX.X, ALU.max)
                    dve.drain()
                    dve.tensor_scalar(small[:, 8:9], small[:, 9:10], -1.0, None, ALU.mult).then_inc(max_ready, 1)
                    split_ahead(pr, 4, L, p)
                    for e in range(2):
                        dve.wait_ge(free(10 + 2 * e), pr.turn(10 + 2 * e, L, p) + 1)
                        dve.reciprocal(small[:, 40 + 4 * e:44 + 4 * e], small[:, 16 + 4 * e:20 + 4 * e])
                        dve.drain()
                        for qb in range(QB):
                            off, n = (0, P, 3 * P, 6 * P)[qb], (qb + 1) * P
                            ins = dve.tensor_scalar(prob[e][:, off:off + n], prob[e][:, off:off + n], small[:, 40 + 4 * e + qb:41 + 4 * e + qb], None, ALU.mult)
                        ins.then_inc(prob_ready, 1)
                    dve.wait_ge(exp_ready, it + 1)
                    dve.reciprocal(small[:, 10:11], small[:, 24:25])
                    dve.drain()
                    dve.tensor_scalar(probs[:], probs[:], small[:, 10:11], None, ALU.mult).then_inc(prob_ready, 1)

                    dve.tensor_tensor(chunk(o, p + 4), chunk(o, p + 4), norm[:, 0:N], ALU.mult).then_inc(by_ready, 1)
                    sc_ = tmp[5]
                    dve.wait_ge(free(6), pr.turn(6, L, p) + 1)
                    dve.tensor_tensor(sc_[:, 0:N], sc_[:, 0:N], norm[:, 0:N], ALU.mult)
                    dve.drain()
                    dve.tensor_tensor(sc_[:, 0:N], sc_[:, 0:N], norm[:, 0:N], ALU.mult)
                    dve.drain()
                    wait_tile(pr, 14, L, p)
                    sx = ps[pr.slot(14)]
                    dve.memset(u[:, 0:HC_], 0.0)
                    cseq = u[:, SC0:SC0 + SB * STEP_C].rearrange("p (s c) -> p s c", c=STEP_C)
                    dve.tensor_tensor(u[:, HC_:HC_ + HF], sc_[:, 0:HF], sx[:, 0, 0:HF], ALU.mult)
                    dve.tensor_tensor(u[:, HC_ + HF:HC_ + SEQ], sc_[:, HF:SEQ], sx[:, 1, 0:SEQ - HF], ALU.mult)
                    dve.tensor_copy(cseq[:, :, 0:HC_], prow[:, R_SS:R_SS + SB * HC_].rearrange("p (s r) -> p s r", r=HC_))
                    dve.tensor_tensor(cseq[:, :, HC_:STEP_C], sc_[:, SEQ:N].rearrange("p (s t) -> p s t", t=ST),
                                      sx[:, 1, SEQ - HF:HF].rearrange("p (s t) -> p s t", t=ST), ALU.mult).then_inc(free(14), 1)
                    dve.drain()
                    uc = kpt
                    taps(uc, u, XCW, R_SW, CONV_C, None)
                    dve.tensor_copy(fcol[:, O_SP:O_SP + HC_], u[:, SEQ:SEQ + HC_])
                    dve.tensor_copy(fcol[:, O_SS:O_SS + SB * HC_].rearrange("p (s r) -> p s r", r=HC_), cseq[:, :, ST:STEP_C])
                    split_ahead(pr, 5, L, p)

                    A, I_, R_, T_, XC_ = tmp[0], tmp[1], tmp[4], tmp[5], tmp[3]
                    dve.wait_ge(gates_ready, it + 1)
                    dve.scalar_tensor_tensor(out=T_[:, 0:XB], in0=R_[:, 0:XB], scalar=1.0, in1=T_[:, 0:XB], op0=ALU.add, op1=ALU.mult)\
                        .then_inc(root_in, 1)
                    dve.tensor_tensor(I_[:, 0:XB], I_[:, 0:XB], XC_[:, 0:XB], ALU.mult)
                    wait_tile(pr, 20, L, p)
                    sbp = ps[pr.slot(20)]
                    oc = o[:, bass.ds(p + 8, 1), :].rearrange("p a n -> p (a n)")
                    dve.tensor_tensor(oc[:, 0:HF], uc[:, 0:HF], sbp[:, 0, 0:HF], ALU.mult)
                    dve.tensor_tensor(oc[:, HF:SEQ], uc[:, HF:SEQ], sbp[:, 1, 0:SEQ - HF], ALU.mult)
                    ocs = o[:, bass.ds(p + 8, 1), SEQ:N].rearrange("p a (s t) -> p (a s) t", t=ST)
                    dve.tensor_tensor(ocs, sequences(uc, SC0, STEP_C, 0, ST), sbp[:, 1, SEQ - HF:HF].rearrange("p (s t) -> p s t", t=ST), ALU.mult).then_inc(free(20), 1)
                    split_ahead(pr, 6, L, p)
                    split_ahead(pr, 7, L, p)
                    dve.drain()
                    dve.wait_ge(root_ready, it + 1)
                    dve.tensor_tensor(I_[:, 0:XB], I_[:, 0:XB], T_[:, 0:XB], ALU.mult)

                    dve.tensor_tensor(small[:, 48:56], one_each(A, 0), prow[:, R_H0:R_H0 + SB], ALU.mult)
                    dve.drain()
                    dve.tensor_tensor(one_each(I_, 0), one_each(I_, 0), small[:, 48:56], ALU.add)
                    dve.memset(one_each(A, 0), 0.0)
                    dve.drain()
                    dve.tensor_tensor_scan(R_[:, 0:XB], A[:, 0:XB], I_[:, 0:XB], 0.0, ALU.mult, ALU.add)
                    dve.drain()
                    dve.wait_ge(gelu_ready, it + 1)
                    og = o[:, bass.ds(p + 4, 1), :].rearrange("p a n -> p (a n)")
                    dve.tensor_tensor(og[:, 0:SEQ], R_[:, 0:SEQ], og[:, 0:SEQ], ALU.mult)
                    ogs = o[:, bass.ds(p + 4, 1), SEQ:N].rearrange("p a (s t) -> p (a s) t", t=ST)
                    dve.tensor_tensor(ogs, sequences(R_, SB0, STEP_B, 0, ST), ogs, ALU.mult)
                    dve.tensor_copy(fcol[:, O_HP:O_HP + 1], R_[:, SEQ - 1:SEQ])
                    dve.tensor_copy(fcol[:, O_HS:O_HS + SB], one_each(R_, ST - 1))
                    dve.drain()
                    dve.tensor_tensor(oc, oc, norm[:, 0:N], ALU.mult)
                    dve.tensor_copy(fout[:, bass.ds(p, 1), :].rearrange("p a n -> p (a n)"), fcol[:])
                    dve.drain()
                dve.drain().then_inc(f_ready, 1)

                dve.wait_ge(v_stored, L * 32 + 32)
                dve.wait_ge(lf_stored, L * 32 + 32)
                dve.wait_ge(k_stored, L * (PAIRS * 32) + PAIRS * 32)
                for c in range(12):
                    dve.wait_ge(oh_ready, L * 12 + (c + 1))
                    dve.tensor_tensor(ol[:, c, :], o[:, c, :], oh[:, c, :].bitcast(F32), ALU.subtract).then_inc(o_ready, 1)
                mg = S["merge"]
                with dve.Fori(0, mg.steps) as i:
                    for b in range(3):
                        for j in range(4):
                            k = 4 * b + j
                            split_ahead(mg, k, L, i)
                            wait_tile(mg, k, L, i)
                            if j < 2:
                                dve.tensor_tensor(two(tmp[j][:, 0:N]), cols(mg.slot(k)), two(tmp[6][:, 0:N]), ALU.mult)\
                                    .then_inc(freed[mg.slot(k)], 1)
                                continue
                            dve.wait_ge(gate_ready, L * 24 + i * 6 + (2 * b + j - 1))
                            mt = merged[:, bass.ds(i * 2 + (j - 2), 1), :].rearrange("p a (b n) -> p (a b) n", b=2)
                            if b == 0:
                                dve.tensor_tensor(mt, two(tmp[j - 2][:, 0:N]), cols(mg.slot(k)), ALU.mult).then_inc(freed[mg.slot(k)], 1)
                                dve.drain()
                            else:
                                t = two(tmp[2 + j][:, 0:N])
                                dve.tensor_tensor(t, two(tmp[j - 2][:, 0:N]), cols(mg.slot(k)), ALU.mult).then_inc(freed[mg.slot(k)], 1)
                                dve.drain()
                                dve.tensor_tensor(mt, mt, t, ALU.add)
                            if b == 2:
                                c = i * 2 + (j - 2)
                                dve.drain()
                                dve.tensor_copy(chunk(mh, c), chunk(merged, c))
                                dve.drain()
                                dve.tensor_tensor(chunk(ml, c), chunk(merged, c), chunk(mh, c).bitcast(F32), ALU.subtract).then_inc(m_ready, 1)
                update(S["out"], L, 1.0, 16, L, 16)
                ffn("ffn2", 2, L)
                dve.wait_ge(f_stored, L * 96 + 96)

        @block.gpsimd
        def _(pool):
            def add_squares(base):
                for m in range(KD):
                    if m == 0:
                        wait_apart(pool, sq_ready, base + (m + 1))
                        pool.tensor_copy(tmp[6][:, 0:N], tmp[2][:, 0:N]).then_inc(sq_added, 1)
                    else:
                        pool.drain()
                        pool.wait_ge(sq_ready, base + (m + 1))
                        pool.tensor_tensor(tmp[6][:, 0:N], tmp[6][:, 0:N], tmp[2 + m % 2][:, 0:N], ALU.add).then_inc(sq_added, 1)

            add_squares(0)
            with pool.Fori(0, DEPTH) as L:
                add_squares(L * 24 + 8)
                fv, pr, st = S["fv"], S["pair"], S["state"]
                for k in (1, 2, 4, 5):
                    wait_apart(pool, freed[fv.slot(k)], fv.turn(k, L) + 1)
                dst = t_out["prompt_v"].rearrange("a l (b p) h d -> l p (a b) (h d)", p=P)[bass.ds(L, 1)]
                pool.dma_start(dst.rearrange("l p b n -> p (l b) n"), vtok[:, 0:4, :]).then_inc(v_stored, 16)
                dst = t_out["sample_v"].rearrange("s l t h d -> l s t (h d)")[bass.ds(L, 1)].rearrange("l s t n -> (l s) t n")
                pool.dma_start(dst, vtok[NS:P, 4, :]).then_inc(v_stored, 16)
                wait_apart(pool, freed[fv.slot(7)], fv.turn(7, L) + 1)
                dst = t_out["prompt_logf"].rearrange("a l (b p) h -> l p (a b) h", p=P)[bass.ds(L, 1)]
                pool.dma_start(dst.rearrange("l p b n -> p (l b) n"), lfo[:, 0:4, :]).then_inc(lf_stored, 16)
                dst = t_out["sample_logf"].rearrange("s l t h -> l s t h")[bass.ds(L, 1)].rearrange("l s t n -> (l s) t n")
                pool.dma_start(dst, lfo[NS:P, 4, :]).then_inc(lf_stored, 16)
                with pool.Fori(0, PAIRS) as p:
                    wait_apart(pool, filled[pr.slot(13)], pr.turn(13, L, p) + 1)
                    pool.tensor_copy(vp[:], vtok[:, :, bass.ds(p * P, P)]).then_inc(vp_ready, 1)
                    wait_apart(pool, freed[pr.slot(13)], pr.turn(13, L, p) + 1)
                    dst = t_out["prompt_k"].rearrange("a l (b p) h d -> l p (a b) (h d)", p=P)[bass.ds(L, 1), :, :, bass.ds(p * P, P)]
                    pool.dma_start(dst.rearrange("l p b n -> p (l b) n"), kout[:, 0:4, :]).then_inc(k_stored, 16)
                    dst = t_out["sample_k"].rearrange("s l t h d -> l s t (h d)")[bass.ds(L, 1), :, :, bass.ds(p * P, P)]
                    pool.dma_start(dst.rearrange("l s t n -> (l s) t n"), kout[NS:P, 4, :])\
                        .then_inc(k_stored, 16)
                wait_apart(pool, freed[st.slot(0)], st.turn(0, L) + 1)
                for name, r, n in (("prompt_lru_h", O_HP, 1), ("prompt_lru_conv", O_CP, HB_), ("prompt_sc_conv", O_SP, HC_),
                                   ("sample_lru_h", O_HS, SB), ("sample_lru_conv", O_CS, HB_), ("sample_sc_conv", O_SS, HC_)):
                    out = t_out[name]
                    if len(out.shape) == 3:
                        dst = out[:, bass.ds(L, 1), :].rearrange("s l n -> (s l) n")
                        pool.dma_start(dst, frow[r:r + n, :]).then_inc(f_stored, 16)
                    elif name.startswith("prompt"):
                        dst = out[:, bass.ds(L, 1), :, :].rearrange("s l r n -> (s l r) n")
                        pool.dma_start(dst, frow[r:r + n, :]).then_inc(f_stored, 16)
                    else:
                        dst = out[:, bass.ds(L, 1), :, :].rearrange("s l r n -> (s l) r n")
                        pool.dma_start(dst, frow[r:r + n * SB, :]).then_inc(f_stored, 16)
                add_squares(L * 24 + 16)
                add_squares(L * 24 + 24)




def constants():
    c = np.zeros((P, NCONST), np.float32)
    r = np.arange(P)
    c[:, C_ID:C_ID + P] = np.eye(P)
    c[:, C_ONE:C_ONE + P] = 1.0 / D
    c[:, C_BONE:C_BONE + P] = (r[:, None] // HD == r[None] // HD) / HD
    row_s, row_h = r % NS // H, r % H
    col_s, col_h, col_q = r // 16, r // ST % 2, r % ST
    for p in range(PAIRS):
        c[:, C_IND + p * P:C_IND + (p + 1) * P] = (row_s[:, None] == col_s) & (row_h[:, None] == 2 * p + col_h)
    n = np.arange(NS)
    c[:, C_MREP:C_MREP + NS] = row_s[:, None] == n // ST
    c[:H, C_REP:C_REP + P] = np.arange(H)[:, None] == r % H
    part = r % 32
    for h in range(H):
        c[:96, C_SEL + 2 * h] = (part == H + h)[:96]
        c[:96, C_SEL + 2 * h + 1] = (part == h)[:96]
    c[:96, C_M12] = -(part < H)[:96].astype(np.float32)
    c[:96, C_M12 + 1] = ((part >= H) & (part < 2 * H))[:96]
    c[:, C_MD:C_MD + P] = np.where(r[None] <= r[:, None], 0.0, NEG)
    key_s, key_t = (r - NS) // ST, (r - NS) % ST
    seen = (r[None] >= NS) & (key_s[None] == col_s[:, None]) & (key_t[None] <= col_q[:, None])
    c[:, C_MS:C_MS + P] = np.where(seen, 0.0, NEG)
    return c


_OUTS = [
    ("y_prompt", (1, SEQ, D)), ("y_sample", (SB, ST, D)),
    ("prompt_k", (1, DEPTH, SEQ, H, HD)), ("prompt_v", (1, DEPTH, SEQ, H, HD)), ("prompt_logf", (1, DEPTH, SEQ, H)),
    ("prompt_lru_h", (1, DEPTH, WID)), ("prompt_lru_conv", (1, DEPTH, HB_, WID)), ("prompt_sc_conv", (1, DEPTH, HC_, WID)),
    ("sample_k", (SB, DEPTH, ST, H, HD)), ("sample_v", (SB, DEPTH, ST, H, HD)), ("sample_logf", (SB, DEPTH, ST, H)),
    ("sample_lru_h", (SB, DEPTH, WID)), ("sample_lru_conv", (SB, DEPTH, HB_, WID)), ("sample_sc_conv", (SB, DEPTH, HC_, WID)),
]


def kernel(**inputs):
    import numpy as _np
    import concourse.bacc as _bacc
    from concourse import mybir as _mybir
    from concourse.bass_utils import run_bass_kernel_spmd as _run

    nc = _bacc.Bacc("TRN2", target_bir_lowering=False, num_devices=1)
    arrays = {f"in_{name}": _np.ascontiguousarray(a) for name, a in inputs.items()}
    arrays["in_const_table"] = constants()
    t_in = {name[3:]: nc.dram_tensor(name, a.shape, _mybir.dt.from_np(a.dtype), kind="ExternalInput").ap()
            for name, a in arrays.items()}
    t_out = {name: nc.dram_tensor(f"out_{name}", shape, _mybir.dt.float32, kind="ExternalOutput").ap()
             for name, shape in _OUTS}
    build(nc, t_in, t_out)
    r = _run(nc, [arrays], core_ids=[0])
    return tuple(r.results[0][f"out_{name}"] for name, _ in _OUTS)
```
